# Optimizing a Trainium2 kernel written in Bass

```python
import math
import jax, jax.numpy as jnp
from jax import lax
import numpy as np

D_MODEL = 1024
BATCH = 1
SEQ = 512
DEPTH = 1
DEC_BATCH = 8
DEC_SEQ = 1
PAST_LEN = 1024
PAGE_SIZE = 128

SSD_EXPAND = 2
D_INNER = SSD_EXPAND * D_MODEL
SSD_HEAD_DIM = 64
SSD_HEADS = D_INNER // SSD_HEAD_DIM
SSD_GROUPS = 4
SSD_STATE = 128
CONV_W = 4
CONV_DIM = D_INNER + 2 * SSD_GROUPS * SSD_STATE
SSD_CHUNK = 128
DT_MIN = 0.001
DT_MAX = 0.1
N_HEADS = 16
N_KV_HEADS = 4
HEAD_DIM = 64
ATTN_WIDTH = N_HEADS * HEAD_DIM
KV_WIDTH = N_KV_HEADS * HEAD_DIM
IDX_HEADS = 8
IDX_DIM = 64
IDX_SCALE = (IDX_HEADS ** -0.5) * (IDX_DIM ** -0.5)
TOPK_MAX = 256
ROPE_THETA = 10000.0
Q_BLOCK = 128
D_FF = ((8 * D_MODEL // 3 + 255) // 256) * 256
EPS = 1e-6
IN_SIZES = (D_INNER, CONV_DIM, SSD_HEADS, ATTN_WIDTH, KV_WIDTH, KV_WIDTH,
            IDX_HEADS * IDX_DIM, IDX_DIM, IDX_HEADS, D_MODEL, D_MODEL)
N_IN = sum(IN_SIZES)

kernel_name = "hybrid_ssd_dsa_gated_decoder_step"

def rmsnorm(x, g):
    xf = x.astype(jnp.float32)
    y = xf * lax.rsqrt(jnp.mean(xf * xf, axis=-1, keepdims=True) + EPS)
    return (y * g.astype(jnp.float32)).astype(x.dtype)

def layernorm(x, g, b):
    xf = x.astype(jnp.float32)
    mu = jnp.mean(xf, axis=-1, keepdims=True)
    var = jnp.mean((xf - mu) ** 2, axis=-1, keepdims=True)
    y = (xf - mu) * lax.rsqrt(var + EPS) * g.astype(jnp.float32) + b.astype(jnp.float32)
    return y.astype(x.dtype)

def gated_rmsnorm(y, z, g):
    u = (y * jax.nn.silu(z)).astype(jnp.float32)
    shp = u.shape
    u = u.reshape(shp[:-1] + (SSD_GROUPS, shp[-1] // SSD_GROUPS))
    u = u * lax.rsqrt(jnp.mean(u * u, axis=-1, keepdims=True) + EPS)
    return (u.reshape(shp) * g.astype(jnp.float32)).astype(y.dtype)

def rope(x, pos):
    d = x.shape[-1]
    half = d // 2
    inv = ROPE_THETA ** (-(jnp.arange(half, dtype=jnp.float32) * 2.0) / d)
    ang = pos.astype(jnp.float32)[:, None] * inv[None, :]
    cos = jnp.cos(ang)[None, :, None, :]
    sin = jnp.sin(ang)[None, :, None, :]
    x1 = x[..., :half].astype(jnp.float32)
    x2 = x[..., half:].astype(jnp.float32)
    out = jnp.concatenate([x1 * cos - x2 * sin, x2 * cos + x1 * sin], axis=-1)
    return out.astype(x.dtype)

def split_columns(u):
    cuts = tuple(int(c) for c in np.cumsum(IN_SIZES)[:-1])
    return jnp.split(u, cuts, axis=-1)

def project(x, pos, g_pre, w_in, g_ik, b_ik):
    bsz, t = x.shape[0], x.shape[1]
    h = rmsnorm(x, g_pre)
    u = h @ w_in
    z, xbc, dt_raw, q, k, v, qi, ki, wi, ga, gb = split_columns(u)
    q = rope(q.reshape(bsz, t, N_HEADS, HEAD_DIM), pos)
    k = rope(k.reshape(bsz, t, N_KV_HEADS, HEAD_DIM), pos)
    v = v.reshape(bsz, t, N_KV_HEADS, HEAD_DIM)
    qi = rope(qi.reshape(bsz, t, IDX_HEADS, IDX_DIM), pos)
    ki = rope(layernorm(ki, g_ik, b_ik)[:, :, None, :], pos)[:, :, 0, :]
    return z, xbc, dt_raw, q, k, v, qi, ki, wi, ga, gb

def causal_conv(xbc, buf, w, b):
    t = xbc.shape[1]
    xp = jnp.concatenate([buf.astype(xbc.dtype), xbc], axis=1)
    out = b
    for j in range(CONV_W):
        out = out + w[j] * xp[:, j:j + t]
    return out, xp[:, -(CONV_W - 1):]

def ssd_prep(xbc_conv, dt_raw, dt_bias, a_log):
    bsz, t = xbc_conv.shape[0], xbc_conv.shape[1]
    xbc = jax.nn.silu(xbc_conv)
    xs, bs, cs = jnp.split(xbc, [D_INNER, D_INNER + SSD_GROUPS * SSD_STATE], axis=-1)
    xs = xs.reshape(bsz, t, SSD_HEADS, SSD_HEAD_DIM)
    bs = bs.reshape(bsz, t, SSD_GROUPS, SSD_STATE)
    cs = cs.reshape(bsz, t, SSD_GROUPS, SSD_STATE)
    dt = jax.nn.softplus((dt_raw + dt_bias).astype(jnp.float32))
    a = -jnp.exp(a_log.astype(jnp.float32))
    return xs, bs, cs, dt, a

def ssd_chunked(xs, dt, a, bs, cs):
    bsz, s = xs.shape[0], xs.shape[1]
    q = SSD_CHUNK
    nc = s // q
    r = SSD_HEADS // SSD_GROUPS
    xr = xs.reshape(bsz, nc, q, SSD_GROUPS, r, SSD_HEAD_DIM)
    dtr = dt.reshape(bsz, nc, q, SSD_GROUPS, r)
    br = bs.reshape(bsz, nc, q, SSD_GROUPS, SSD_STATE)
    cr = cs.reshape(bsz, nc, q, SSD_GROUPS, SSD_STATE)
    cum = jnp.cumsum(dtr * a.reshape(SSD_GROUPS, r), axis=2)
    causal = jnp.tril(jnp.ones((q, q), dtype=bool))[:, :, None, None]
    seg = cum[:, :, :, None] - cum[:, :, None, :]
    decay = jnp.exp(jnp.where(causal, seg, -jnp.inf))
    xdt = xr * dtr[..., None]
    cb = jnp.einsum("bclgn,bcsgn->bclsg", cr, br)
    y_diag = jnp.einsum("bclsg,bclsgr,bcsgrp->bclgrp", cb, decay, xdt)
    decay_last = jnp.exp(cum[:, :, -1:] - cum)
    chunk_states = jnp.einsum("bcsgn,bcsgr,bcsgrp->bcgrpn", br, decay_last, xdt)
    chunk_decay = jnp.exp(cum[:, :, -1])

    def step(h, inp):
        st, dec = inp
        return dec[..., None, None] * h + st, h

    h0 = jnp.zeros((bsz, SSD_GROUPS, r, SSD_HEAD_DIM, SSD_STATE), chunk_states.dtype)
    h_final, h_starts = lax.scan(step, h0, (jnp.moveaxis(chunk_states, 1, 0), jnp.moveaxis(chunk_decay, 1, 0)))
    h_starts = jnp.moveaxis(h_starts, 0, 1)
    y_off = jnp.einsum("bclgn,bcgrpn,bclgr->bclgrp", cr, h_starts, jnp.exp(cum))
    y = (y_diag + y_off).reshape(bsz, s, SSD_HEADS, SSD_HEAD_DIM)
    return y, h_final.reshape(bsz, SSD_HEADS, SSD_HEAD_DIM, SSD_STATE)

def ssd_recurrent(xs, dt, a, bs, cs, h0):
    bsz, t = xs.shape[0], xs.shape[1]
    r = SSD_HEADS // SSD_GROUPS
    ar = a.reshape(SSD_GROUPS, r)
    xr = jnp.moveaxis(xs.reshape(bsz, t, SSD_GROUPS, r, SSD_HEAD_DIM), 1, 0)
    dtr = jnp.moveaxis(dt.reshape(bsz, t, SSD_GROUPS, r), 1, 0)
    br = jnp.moveaxis(bs, 1, 0)
    cr = jnp.moveaxis(cs, 1, 0)

    def step(h, inp):
        xt, dtt, bt, ct = inp
        h = jnp.exp(dtt * ar)[..., None, None] * h + jnp.einsum("bgrp,bgn,bgr->bgrpn", xt, bt, dtt)
        return h, jnp.einsum("bgrpn,bgn->bgrp", h, ct)

    h_init = h0.astype(jnp.float32).reshape(bsz, SSD_GROUPS, r, SSD_HEAD_DIM, SSD_STATE)
    h, ys = lax.scan(step, h_init, (xr, dtr, br, cr))
    y = jnp.moveaxis(ys, 0, 1).reshape(bsz, t, SSD_HEADS, SSD_HEAD_DIM)
    return y, h.reshape(bsz, SSD_HEADS, SSD_HEAD_DIM, SSD_STATE)

def ssd_finish(y, xs, z, d_skip, g_ssd):
    bsz, t = xs.shape[0], xs.shape[1]
    y = y.astype(xs.dtype) + d_skip[:, None].astype(xs.dtype) * xs
    return gated_rmsnorm(y.reshape(bsz, t, D_INNER), z, g_ssd)

def indexer_scores(qi, ki, wi):
    dots = jax.nn.relu(jnp.einsum("bthd,bsd->bths", qi, ki).astype(jnp.float32))
    return jnp.einsum("bths,bth->bts", dots, wi.astype(jnp.float32) * IDX_SCALE)

def attend_selected(q, ks, vs, valid):
    bsz, t = q.shape[0], q.shape[1]
    qg = q.reshape(bsz, t, N_KV_HEADS, N_HEADS // N_KV_HEADS, HEAD_DIM)
    logits = jnp.einsum("btgrd,btkgd->btgrk", qg, ks).astype(jnp.float32) * (HEAD_DIM ** -0.5)
    logits = jnp.where(valid[:, :, None, None, :], logits, -jnp.inf)
    p = jax.nn.softmax(logits, axis=-1).astype(vs.dtype)
    o = jnp.einsum("btgrk,btkgd->btgrd", p, vs)
    return o.reshape(bsz, t, ATTN_WIDTH)

def gather_rows(rows, idx):
    return jax.vmap(lambda rr, ii: rr[ii])(rows, idx)

def dsa_prompt(q, k, v, qi, ki, wi):
    bsz, s = q.shape[0], q.shape[1]
    topk = min(TOPK_MAX, s // 4)
    key_pos = jnp.arange(s)

    def block(start):
        qb = lax.dynamic_slice_in_dim(q, start, Q_BLOCK, axis=1)
        qib = lax.dynamic_slice_in_dim(qi, start, Q_BLOCK, axis=1)
        wib = lax.dynamic_slice_in_dim(wi, start, Q_BLOCK, axis=1)
        qpos = start + jnp.arange(Q_BLOCK)
        sc = indexer_scores(qib, ki, wib)
        sc = jnp.where((key_pos[None, :] <= qpos[:, None])[None], sc, -jnp.inf)
        _, sel = lax.top_k(sc, topk)
        valid = sel <= qpos[None, :, None]
        return attend_selected(qb, gather_rows(k, sel), gather_rows(v, sel), valid)

    out = lax.map(block, jnp.arange(0, s, Q_BLOCK))
    return jnp.moveaxis(out, 0, 1).reshape(bsz, s, ATTN_WIDTH)

def dsa_sample(q, k_new, v_new, qi, ki_new, wi, cache_k, cache_v, cache_idx_k, page_table, layer):
    bsz, t = q.shape[0], q.shape[1]
    n_pages = page_table.shape[1]
    past = n_pages * PAGE_SIZE
    total = past + t
    topk = min(TOPK_MAX, total // 4)
    past_ki = cache_idx_k[layer, page_table].reshape(bsz, past, IDX_DIM)
    all_ki = jnp.concatenate([past_ki.astype(ki_new.dtype), ki_new], axis=1)
    sc = indexer_scores(qi, all_ki, wi)
    qpos = past + jnp.arange(t)
    sc = jnp.where((jnp.arange(total)[None, :] <= qpos[:, None])[None], sc, -jnp.inf)
    _, sel = lax.top_k(sc, topk)
    valid = sel <= qpos[None, :, None]
    in_past = sel < past
    sel_p = jnp.minimum(sel, past - 1)
    phys = jnp.take_along_axis(page_table, (sel_p // PAGE_SIZE).reshape(bsz, -1), axis=1).reshape(sel.shape)
    off = sel_p % PAGE_SIZE
    new_idx = jnp.clip(sel - past, 0, t - 1)
    ks = jnp.where(in_past[..., None, None], cache_k[layer, phys, off].astype(k_new.dtype), gather_rows(k_new, new_idx))
    vs = jnp.where(in_past[..., None, None], cache_v[layer, phys, off].astype(v_new.dtype), gather_rows(v_new, new_idx))
    return attend_selected(q, ks, vs, valid)

def merge_and_ffn(x, y_ssd, y_attn, ga, gb, w_ssd_out, w_attn_out, w_o, g_mix_post, g_ffn_pre, w_gate_up, w_down, g_ffn_post):
    mixed = jax.nn.sigmoid(ga) * (y_ssd @ w_ssd_out) + jax.nn.sigmoid(gb) * (y_attn @ w_attn_out)
    x = x + rmsnorm(mixed @ w_o, g_mix_post)
    gate, up = jnp.split(rmsnorm(x, g_ffn_pre) @ w_gate_up, 2, axis=-1)
    return x + rmsnorm((jax.nn.silu(gate) * up) @ w_down, g_ffn_post)

def setup_inputs(seed: int = 0) -> dict:
    key = jax.random.key(seed)
    ks = jax.random.split(key, 32)
    f32 = jnp.float32
    n_pages = PAST_LEN // PAGE_SIZE
    n_used = DEC_BATCH * n_pages
    n_pool = n_used + n_used // 4

    def nrm(k, shape, scale):
        return scale * jax.random.normal(k, shape, f32)

    dt0 = jnp.exp(jax.random.uniform(ks[14], (DEPTH, SSD_HEADS), f32, math.log(DT_MIN), math.log(DT_MAX)))
    return {
        "x_prompt": nrm(ks[0], (BATCH, SEQ, D_MODEL), 1.0),
        "x_sample": nrm(ks[1], (DEC_BATCH, DEC_SEQ, D_MODEL), 1.0),
        "cache_k": nrm(ks[2], (DEPTH, n_pool, PAGE_SIZE, N_KV_HEADS, HEAD_DIM), 1.0),
        "cache_v": nrm(ks[3], (DEPTH, n_pool, PAGE_SIZE, N_KV_HEADS, HEAD_DIM), 1.0),
        "cache_idx_k": nrm(ks[4], (DEPTH, n_pool, PAGE_SIZE, IDX_DIM), 1.0),
        "state_ssm": nrm(ks[5], (DEPTH, DEC_BATCH, SSD_HEADS, SSD_HEAD_DIM, SSD_STATE), 0.1),
        "state_conv": nrm(ks[6], (DEPTH, DEC_BATCH, CONV_W - 1, CONV_DIM), 1.0),
        "page_table": jax.random.permutation(ks[7], n_pool)[:n_used].reshape(DEC_BATCH, n_pages).astype(jnp.int32),
        "g_mix_pre": 1.0 + nrm(ks[8], (DEPTH, D_MODEL), 0.05),
        "w_in": nrm(ks[9], (DEPTH, D_MODEL, N_IN), D_MODEL ** -0.5),
        "g_idx_k": 1.0 + nrm(ks[10], (DEPTH, IDX_DIM), 0.05),
        "b_idx_k": nrm(ks[11], (DEPTH, IDX_DIM), 0.01),
        "conv_w": nrm(ks[12], (DEPTH, CONV_W, CONV_DIM), CONV_W ** -0.5),
        "conv_b": nrm(ks[13], (DEPTH, CONV_DIM), 0.01),
        "dt_bias": dt0 + jnp.log(-jnp.expm1(-dt0)),
        "a_log": jnp.log(jax.random.uniform(ks[15], (DEPTH, SSD_HEADS), f32, 1.0, 16.0)),
        "d_skip": 1.0 + nrm(ks[16], (DEPTH, SSD_HEADS), 0.1),
        "g_ssd": 1.0 + nrm(ks[17], (DEPTH, D_INNER), 0.05),
        "w_ssd_out": nrm(ks[18], (DEPTH, D_INNER, D_MODEL), D_INNER ** -0.5),
        "w_attn_out": nrm(ks[19], (DEPTH, ATTN_WIDTH, D_MODEL), ATTN_WIDTH ** -0.5),
        "w_o": nrm(ks[20], (DEPTH, D_MODEL, D_MODEL), D_MODEL ** -0.5),
        "g_mix_post": 1.0 + nrm(ks[21], (DEPTH, D_MODEL), 0.05),
        "g_ffn_pre": 1.0 + nrm(ks[22], (DEPTH, D_MODEL), 0.05),
        "w_gate_up": nrm(ks[23], (DEPTH, D_MODEL, 2 * D_FF), D_MODEL ** -0.5),
        "w_down": nrm(ks[24], (DEPTH, D_FF, D_MODEL), D_FF ** -0.5),
        "g_ffn_post": 1.0 + nrm(ks[25], (DEPTH, D_MODEL), 0.05),
    }

def reference(x_prompt, x_sample, cache_k, cache_v, cache_idx_k, state_ssm, state_conv, page_table,
              g_mix_pre, w_in, g_idx_k, b_idx_k, conv_w, conv_b, dt_bias, a_log, d_skip, g_ssd,
              w_ssd_out, w_attn_out, w_o, g_mix_post, g_ffn_pre, w_gate_up, w_down, g_ffn_post):
    bp, sp = x_prompt.shape[0], x_prompt.shape[1]
    ts = x_sample.shape[1]
    past = page_table.shape[1] * PAGE_SIZE
    pos_p = jnp.arange(sp)
    pos_s = past + jnp.arange(ts)
    yp, ys = x_prompt, x_sample
    kp_l, vp_l, ikp_l, ssmp_l, convp_l = [], [], [], [], []
    ks_l, vs_l, iks_l, ssms_l, convs_l = [], [], [], [], []
    for l in range(DEPTH):
        z, xbc, dtr, q, k, v, qi, ki, wi, ga, gb = project(yp, pos_p, g_mix_pre[l], w_in[l], g_idx_k[l], b_idx_k[l])
        xbc_c, conv_p = causal_conv(xbc, jnp.zeros((bp, CONV_W - 1, CONV_DIM), xbc.dtype), conv_w[l], conv_b[l])
        xs, bs, cs, dt, a = ssd_prep(xbc_c, dtr, dt_bias[l], a_log[l])
        y_s, ssm_p = ssd_chunked(xs, dt, a, bs, cs)
        y_ssd = ssd_finish(y_s, xs, z, d_skip[l], g_ssd[l])
        y_attn = dsa_prompt(q, k, v, qi, ki, wi)
        yp = merge_and_ffn(yp, y_ssd, y_attn, ga, gb, w_ssd_out[l], w_attn_out[l], w_o[l],
                           g_mix_post[l], g_ffn_pre[l], w_gate_up[l], w_down[l], g_ffn_post[l])
        kp_l.append(k)
        vp_l.append(v)
        ikp_l.append(ki)
        ssmp_l.append(ssm_p.astype(state_ssm.dtype))
        convp_l.append(conv_p.astype(state_conv.dtype))
        z, xbc, dtr, q, k, v, qi, ki, wi, ga, gb = project(ys, pos_s, g_mix_pre[l], w_in[l], g_idx_k[l], b_idx_k[l])
        xbc_c, conv_s = causal_conv(xbc, state_conv[l], conv_w[l], conv_b[l])
        xs, bs, cs, dt, a = ssd_prep(xbc_c, dtr, dt_bias[l], a_log[l])
        y_s, ssm_s = ssd_recurrent(xs, dt, a, bs, cs, state_ssm[l])
        y_ssd = ssd_finish(y_s, xs, z, d_skip[l], g_ssd[l])
        y_attn = dsa_sample(q, k, v, qi, ki, wi, cache_k, cache_v, cache_idx_k, page_table, l)
        ys = merge_and_ffn(ys, y_ssd, y_attn, ga, gb, w_ssd_out[l], w_attn_out[l], w_o[l],
                           g_mix_post[l], g_ffn_pre[l], w_gate_up[l], w_down[l], g_ffn_post[l])
        ks_l.append(k)
        vs_l.append(v)
        iks_l.append(ki)
        ssms_l.append(ssm_s.astype(state_ssm.dtype))
        convs_l.append(conv_s.astype(state_conv.dtype))
    k_prompt = jnp.stack(kp_l, axis=0)
    v_prompt = jnp.stack(vp_l, axis=0)
    idx_k_prompt = jnp.stack(ikp_l, axis=0)
    ssm_prompt = jnp.stack(ssmp_l, axis=0)
    conv_prompt = jnp.stack(convp_l, axis=0)
    k_sample = jnp.stack(ks_l, axis=0)
    v_sample = jnp.stack(vs_l, axis=0)
    idx_k_sample = jnp.stack(iks_l, axis=0)
    ssm_sample = jnp.stack(ssms_l, axis=0)
    conv_sample = jnp.stack(convs_l, axis=0)
    return (yp, ys, k_prompt, v_prompt, idx_k_prompt, ssm_prompt, conv_prompt,
            k_sample, v_sample, idx_k_sample, ssm_sample, conv_sample)


_drawn_inputs = setup_inputs


def setup_inputs(seed=0):
    import zlib

    import numpy as np

    out = dict(_drawn_inputs(seed))
    spreads = {}
    factors = {'b_idx_k': 5.528, 'conv_b': 3.797}
    for name, (base, spread) in spreads.items():
        noise = np.random.default_rng([zlib.crc32(name.encode()), seed]).standard_normal(out[name].shape)
        drawn = base * np.exp(spread * noise) if base else spread * noise
        out[name] = __import__('jax').numpy.asarray(drawn.astype(out[name].dtype))
    for name, factor in factors.items():
        out[name] = (out[name] * factor).astype(out[name].dtype)
    return out
```

```python
from contextlib import ExitStack

import concourse.bass as bass
import numpy as np
from concourse import mybir

F32 = mybir.dt.float32
F32R = mybir.dt.float32r
I32 = mybir.dt.int32
ALU = mybir.AluOpType
ACT = mybir.ActivationFunctionType
AX_X = mybir.AxisListType.X

P = 128
D = 1024
TP = 512
NS = 8
T = TP + NS
HB = T // 2
NBLK = TP // P
KD = D // P
PAST, PAGE = 1024, 128
NPG = PAST // PAGE
DI = 2 * D
HS, HDS, GS, NST = 32, 64, 4, 128
RH = HS // GS
CW = 4
CD = DI + 2 * GS * NST
NX = DI // P
NC = CD // P
NH, NKV, HD = 16, 4, 64
AW, KW = NH * HD, NKV * HD
NQ = AW // P
IH, IDM = 8, 64
NI = IH * IDM // P
IDX_SCALE = (IH ** -0.5) * (IDM ** -0.5)
SM_SCALE = HD ** -0.5
TOPK_P = min(256, TP // 4)
TOPK_S = min(256, (PAST + 1) // 4)
DFF = ((8 * D // 3 + 255) // 256) * 256
NF = DFF // P
EPS = 1e-6
NEG = -1.0e30
GONE = -3.0e38
C_Z = 0
C_XBC = DI
C_DT = C_XBC + CD
C_Q = C_DT + HS
C_K = C_Q + AW
C_V = C_K + KW
C_QI = C_V + KW
C_KI = C_QI + IH * IDM
C_GA = C_KI + IDM + IH
C_GB = C_GA + D
NMISC = IDM + IH + HS

U_T, U_Q, U_X, U_Z, U_G = 0, 5, 5 + NI + NQ, 5 + NI + NQ + NC, 5 + NI + NQ + NC + NX
U_SO = U_G + 2 * KD
U_AO = U_SO + 2 * KD
U_WO = U_AO + KD
U_GU = U_WO + KD
U_DN = U_GU + 2 * NF
U_END = U_DN + 3 * KD
O_X0 = 0
O_T = KD
O_Q = O_T + 5
O_X = O_Q + NI + NQ
O_Z = O_X + NC
O_G = O_Z + NX
O_SO = O_G + 2 * KD
O_AO = O_SO + KD
O_WO = O_AO + KD
O_GU = O_WO + KD
O_DN = O_GU + 2 * NF
L_Y, L_A, L_M, L_F, L_AH = KD, KD + NX, KD + NX + NQ, 2 * KD + NX + NQ, 3 * KD + NX + NQ
N_Y, N_O, N_D = KD, KD + NX, 2 * KD + NX
Q_O, Q_X, Q_D = KD, 2 * KD, 3 * KD
STEP_UNIT = {st: n for n, st in enumerate([st for st in range(GS * NBLK) if st >= 1 and st not in (5, 8)], 2)}
BEFORE = tuple(range(2))
AFTER = tuple(range(len(BEFORE) + len(STEP_UNIT), 2 * KD))
DN_K = (KD, (NF - KD + 1) // 2, (NF - KD) // 2)

K_ID, K_ONE, K_UT, K_ROT, K_CAUS = 0, P, 2 * P, 3 * P, 4 * P
K_COST = 5 * P
K_SINT = K_COST + T
K_COSK = K_SINT + T
K_SINK = K_COSK + 5 * 32
K_DG = K_SINK + 5 * 32
K_DGN = K_DG + NS
K_END = K_DGN + NS


def constants():
    c = np.zeros((P, K_END), np.float32)
    r = np.arange(P)
    c[:, K_ID:K_ID + P] = np.eye(P)
    c[:, K_ONE:K_ONE + P] = 1.0
    c[:, K_UT:K_UT + P] = r[:, None] <= r[None, :]
    for m in range(P):
        if m % 64 < 32:
            c[m + 32, K_ROT + m] = -1.0
        else:
            c[m - 32, K_ROT + m] = 1.0
    c[:, K_CAUS:K_CAUS + P] = np.where(r[None, :] <= r[:, None], 0.0, NEG)
    inv = np.float32(10000.0) ** (-(np.arange(32, dtype=np.float32) * np.float32(2.0)) / np.float32(64))
    pos = np.concatenate([np.arange(TP), np.full(NS, PAST)]).astype(np.float32)
    ang = (pos[:, None] * inv[None, :]).astype(np.float32)
    cos, sin = np.cos(ang), np.sin(ang)
    c[:, K_COST:K_COST + T] = cos[:, r % 32].T
    c[:, K_SINT:K_SINT + T] = sin[:, r % 32].T
    for b in range(5):
        rows = cos[b * P:(b + 1) * P] if b < 4 else cos[TP:]
        c[:len(rows), K_COSK + 32 * b:K_COSK + 32 * (b + 1)] = rows
        rows = sin[b * P:(b + 1) * P] if b < 4 else sin[TP:]
        c[:len(rows), K_SINK + 32 * b:K_SINK + 32 * (b + 1)] = rows
    for b in range(NS):
        c[b, K_DG + b] = 1.0
    c[:NS, K_DGN:K_DGN + NS] = (c[:NS, K_DG:K_DG + NS] - 1.0) * np.float32(-NEG)
    return c


class Core:

    def __init__(self, nc, ctx):
        base = nc.sbuf_base + (-nc.sbuf_base) % 64

        def at(name, shape, offset, dtype=F32):
            return nc.alloc_sbuf_tensor_at(name, [P] + shape, dtype, offset=base + offset)

        self.raw = at("raw", [2, KD, P], 0)
        self.wh = at("wh", [2, KD, P], 8192, F32R)
        self.wl = at("wl", [2, KD, P], 16384, F32R)
        self.cst = at("cst", [K_END], 24576)
        offset = 24576 + 4 * K_END

        def small(name, cols):
            nonlocal offset
            t = at(name, [cols], offset)
            offset += 4 * cols + (-4 * cols) % 32
            return t

        self.prm = small("prm", 168)
        self.bcp = small("bcp", 224)
        self.rst = small("rst", T)
        self.dts = small("dts", 5 * HS)
        self.dta = small("dta", 5 * HS)
        self.dgm = at("dgm", [P], offset)
        self.cum = small("cum", P)
        self.expc = small("expc", P)
        self.wdec = small("wdec", P)
        self.dec = small("dec", P)
        self.neg_a = small("neg_a", HS)
        self.dcol = small("dcol", NX)
        self.m8 = small("m8", 4 * 8)
        self.thr = small("thr", 16)
        self.qsi = small("qsi", 2 * 64)
        self.qsm = small("qsm", 2 * 64)
        self.wib = small("wib", 64)
        self.wid = small("wid", 64)
        self.wis = small("wis", 5 * IH)
        self.kts = small("kts", 16)
        self.vsn = small("vsn", KW)
        self.ysm = small("ysm", NX * NS)
        self.xds = small("xds", NX * NS)
        self.dtb = small("dtb", NX * NS)
        self.deb = small("deb", NX * NS)
        self.ysq = small("ysq", NX * NS)
        self.msks = small("msks", 72)
        self.sct = small("sct", 72)
        self.eps = small("eps", 1)
        self.zero = small("zero", 1)
        self.mx = small("mx", 8)
        self.nb = small("nb", 8)
        self.sm = small("sm", 8)
        self.ri = small("ri", 8)
        self.cumt = small("cumt", P)
        self.rss = at("rss", [32], offset)
        self.lns = small("lns", 32)
        self.pages = small("pages", 64)
        self.mxb = small("mxb", P)
        self.rsb = small("rsb", P)
        r1 = offset + (-offset) % 64
        r2 = r1 + 33280
        r3 = r2 + 33280
        r5 = r3 + 16640
        r4 = r5 + 22720
        r8 = r4 + 24960
        assert r8 + 33792 <= nc.sbuf_usable_end - base
        self.hh = at("hh", [KD, T], r1, F32R)
        self.hl = at("hl", [KD, T], r1 + 16640, F32R)
        self.xtok = at("xtok", [NBLK, D], r2)
        self.xtoks = at("xtoks", [D], r2 + 16384)
        self.sq = at("sq", [2, T], r2 + 20480)
        self.tmp = at("tmp", [2, T], r2 + 24640)
        self.xT = at("xT", [KD, T], r3)
        self.kvf = at("kvf", [5, T], r2)
        self.ipg = at("ipg", [NS, NPG, IDM], r2 + 10400)
        self.kit = at("kit", [2, NPG // 2, P], r2 + 6144)
        self.rel = at("rel", [2, TP], r2)
        self.rels = at("rels", [NS * NPG * IH], r2 + 4096)
        self.xbc = at("xbc", [NC, T], r2)
        self.ktd = at("ktd", [NKV, T], r5)
        self.kid = at("kid", [T], r5 + 8320)
        self.vtok = at("vtok", [5, KW], r5 + 10400)
        self.misc = at("misc", [5, NMISC], r5 + 15520)
        self.stT = at("stT", [NC, NS * (CW - 1)], r5 + 17600)
        self.tail = at("tail", [NC, CW - 1 + NS], r8 + 32640)
        self.mask = at("mask", [1280], r5 + 17600)
        self.qall = at("qall", [NI + NQ, T], r4)
        self.csr = at("csr", [CD], r8)
        self.ktok = at("ktok", [5, KW], r8)
        self.kdup = at("kdup", [5, NKV, 2, HD], r8 + 5120)
        self.rt = at("rt", [2, 5 * NKV * 32], r8 + 15360)
        self.sp0 = at("sp0", [5 * HS], r8 + 16064)
        self.sp1 = at("sp1", [5 * HS], r8 + 16768)
        self.kln = at("kln", [5, 2, IDM], r8 + 20480)
        self.klt = at("klt", [5, IDM], r8 + 23040)
        self.qraw = at("qraw", [2, T], r8 + 24320)
        self.qt = at("qt", [2, T], r8 + 28480)
        self.sc = at("sc", [3, TP], r8)
        self.wk = at("wk", [3, TP], r8 + 6144)
        self.scs = at("scs", [9 * P], r8 + 12288)
        self.wks = at("wks", [9 * P], r8 + 16896)
        self.bcs = at("bcs", [2 * GS * P], r8 + 16896)
        self.cx = at("cx", [2, CW - 1 + TP + CW * NS], r8 + 21504)
        self.ca = at("ca", [2, TP + CW * NS], r8 + 25888)
        self.tailtok = at("tailtok", [2, 4 * P], r8 + 25920)
        self.sb = at("sb", [4, TP], r8)
        self.pt = at("pt", [4, TP], r8 + 21504)
        self.eqs = at("eqs", [9 * P], r8)
        self.runs = at("runs", [9 * P], r8 + 21504)
        self.bcb = at("bcb", [2 * GS * P], r4)
        self.ST = (at("state0", [8, P], r4 + 4096), at("state1", [8, P], r8 + 8192))
        self.prods = at("prods", [8, P], r8 + 29696)
        self.yat = at("yat", [4 * HD], r5 + 8832)
        self.zst = at("zst", [T], r5 + 15520)
        self.ddb = at("ddb", [NS * 2 * HS], r5 + 15520)
        self.cbm = at("cbm", [P], r5 + 8320)
        self.btok = at("btok", [P], r5 + 8832)
        self.fin = at("fin", [4, P], r5 + 18720)
        self.zg = at("zg", [4, T], r8 + 8704)
        self.CB = [at("cb%d" % n, [RH * P], r8 + off) for n, off in enumerate((4608, 512))]
        self.xdt = at("xdt", [512], r8 + 17024)
        self.xw = at("xw", [512], r8 + 19072)
        self.sy = at("sy", [512], r8 + 21120)
        self.yt = at("yt", [512], r8 + 23168)
        self.hst = at("hst", [512], r8 + 25216)
        self.gsq = at("gsq", [2, 512], r8 + 27264)
        self.gst = at("gst", [T], r8 + 31360)
        self.YHT = [at("y_hi%d" % g, [4, T], off, F32R) for g, off in enumerate((r5, r4, r5 + 10400, r3 + 8320))]
        self.YL = [at("y_lo%d" % g, [4, T], r2 + 8320 * g, F32R) for g in range(GS)]
        self.kst = at("kst", [16, P], r8)
        self.lg = at("lg", [NS * (NPG + 1) * NH], r8 + 16384)
        self.KP = [at("kpg%d" % n, [NPG, KW], off) for n, off in enumerate((r8 + 8192, r3))]
        self.VP = [at("vpg%d" % n, [NPG, KW], off) for n, off in enumerate((r8 + 20992, r1, r8 + 8192, r3, r8))]
        self.mix = at("mix", [KD, T], r1 + 8320)
        self.gl = at("gl", [4, T], r1 + 24960)
        self.yah = at("yah", [NQ, T], r3, F32R)
        self.yal = at("yal", [NQ, T], r4 + 8320, F32R)
        self.mh = at("mh", [KD, T], r8, F32R)
        self.ml = at("ml", [KD, T], r8 + 16640, F32R)
        self.osq = at("osq", [3, T], r1)
        self.osq2 = at("osq2", [2, T], r1 + 6240)
        self.ot = at("ot", [KD, T], r3)
        self.x1 = at("x1", [KD, T], r4 + 8320)
        self.fh = at("fh", [KD, T], r8, F32R)
        self.fl = at("fl", [KD, T], r8 + 16640, F32R)
        self.ah = at("ah", [NF, T], r1, F32R)
        self.al = at("al", [NF, T], r1 + 45760, F32R)
        self.gs = at("gs", [T], r5 + 8320)
        self.up = at("up", [T], r5 + 10400)
        self.dt = at("dt", [KD, T], r8)
        self.dsq = at("dsq", [3, T], r8 + 16640)
        self.yout = at("yout", [10, 4 * P], r1)
        self.ps = ctx.enter_context(nc.psum_tensor("psum", [P, 8, 512], F32))


class Sems:

    def __init__(self, nc, ctx):
        def sem(name):
            return ctx.enter_context(nc.semaphore(name))

        self.acc_made = sem("acc_made")
        self.av_done = sem("av_done")
        self.bcb_in = sem("bcb_in")
        self.blank_made = sem("blank_made")
        self.bounce_in = sem("bounce_in")
        self.bounce_out = sem("bounce_out")
        self.btok_made = sem("btok_made")
        self.ca_made = sem("ca_made")
        self.cb_done = sem("cb_done")
        self.cb_in0 = sem("cb_in0")
        self.cb_in1 = sem("cb_in1")
        self.cbm_made = sem("cbm_made")
        self.const_in = sem("const_in")
        self.conv_made = sem("conv_made")
        self.cs_done = sem("cs_done")
        self.cum_done = sem("cum_done")
        self.cum_made = sem("cum_made")
        self.cx_made = sem("cx_made")
        self.dec_made = sem("dec_made")
        self.dot_done = sem("dot_done")
        self.dt_step_s = sem("dt_step_s")
        self.dt_step_v = sem("dt_step_v")
        self.dve_step = sem("dve_step")
        self.ea_made = sem("ea_made")
        self.eps_made = sem("eps_made")
        self.ew_made = sem("ew_made")
        self.fin_out = sem("fin_out")
        self.g_in0 = sem("g_in0")
        self.g_in1 = sem("g_in1")
        self.g_in2 = sem("g_in2")
        self.g_in3 = sem("g_in3")
        self.g_out = sem("g_out")
        self.glu_made = sem("glu_made")
        self.gsq_ready = sem("gsq_ready")
        self.gss_done = sem("gss_done")
        self.gstd_made = sem("gstd_made")
        self.h_made = sem("h_made")
        self.hd_made = sem("hd_made")
        self.hi_half_made = sem("hi_half_made")
        self.hi_made = sem("hi_made")
        self.hn_made = sem("hn_made")
        self.hst_copied = sem("hst_copied")
        self.hst_done = sem("hst_done")
        self.hst_in0 = sem("hst_in0")
        self.hst_in1 = sem("hst_in1")
        self.idx_in = sem("idx_in")
        self.ipg_copied = sem("ipg_copied")
        self.ipg_done = sem("ipg_done")
        self.isc_done = sem("isc_done")
        self.kdup_made = sem("kdup_made")
        self.ki_made = sem("ki_made")
        self.kst_copied = sem("kst_copied")
        self.kst_done = sem("kst_done")
        self.kstd_made = sem("kstd_made")
        self.kt_copied = sem("kt_copied")
        self.kt_done = sem("kt_done")
        self.kv_made = sem("kv_made")
        self.kv_turned = sem("kv_turned")
        self.lg_copied = sem("lg_copied")
        self.lg_done = sem("lg_done")
        self.lg_step_t = sem("lg_step_t")
        self.lg_step_v = sem("lg_step_v")
        self.lge_made = sem("lge_made")
        self.lo_half_made = sem("lo_half_made")
        self.logit_done = sem("logit_done")
        self.m_made = sem("m_made")
        self.mix_made = sem("mix_made")
        self.msks_made = sem("msks_made")
        self.mskt_done = sem("mskt_done")
        self.nb_made = sem("nb_made")
        self.out_done = sem("out_done")
        self.p_made = sem("p_made")
        self.page_in0 = sem("page_in0")
        self.page_in1 = sem("page_in1")
        self.prm_copied = sem("prm_copied")
        self.prm_done = sem("prm_done")
        self.psum_free0 = sem("psum_free0")
        self.psum_free1 = sem("psum_free1")
        self.pt_copied = sem("pt_copied")
        self.pt_done = sem("pt_done")
        self.q_made = sem("q_made")
        self.qsi_made = sem("qsi_made")
        self.qsm_made = sem("qsm_made")
        self.qt_made = sem("qt_made")
        self.raw_in0 = sem("raw_in0")
        self.raw_in1 = sem("raw_in1")
        self.rel_made = sem("rel_made")
        self.rot_done = sem("rot_done")
        self.rot_free = sem("rot_free")
        self.rss_made = sem("rss_made")
        self.sct_copied = sem("sct_copied")
        self.sct_done = sem("sct_done")
        self.sct_made = sem("sct_made")
        self.sdd_made = sem("sdd_made")
        self.seg_made = sem("seg_made")
        self.sh_made = sem("sh_made")
        self.silu_made = sem("silu_made")
        self.smask_made = sem("smask_made")
        self.split_done = sem("split_done")
        self.sq_added = sem("sq_added")
        self.sq_ready = sem("sq_ready")
        self.ss_done = sem("ss_done")
        self.state_in = sem("state_in")
        self.state_out = sem("state_out")
        self.std_made = sem("std_made")
        self.sv_done = sem("sv_done")
        self.sxt_done = sem("sxt_done")
        self.sy_made = sem("sy_made")
        self.syt_done = sem("syt_done")
        self.tail_copied = sem("tail_copied")
        self.tail_done = sem("tail_done")
        self.tail_made = sem("tail_made")
        self.tail_out0 = sem("tail_out0")
        self.tail_out1 = sem("tail_out1")
        self.tk_max = sem("tk_max")
        self.tk_rep = sem("tk_rep")
        self.tmp_made = sem("tmp_made")
        self.tot_made = sem("tot_made")
        self.u_made = sem("u_made")
        self.unit_done = sem("unit_done")
        self.usq_made = sem("usq_made")
        self.uss_done = sem("uss_done")
        self.v_in0 = sem("v_in0")
        self.v_in1 = sem("v_in1")
        self.v_in2 = sem("v_in2")
        self.v_in3 = sem("v_in3")
        self.v_in4 = sem("v_in4")
        self.var_made = sem("var_made")
        self.wib_copied = sem("wib_copied")
        self.wib_done = sem("wib_done")
        self.wid_made = sem("wid_made")
        self.x1_made = sem("x1_made")
        self.xT_out = sem("xT_out")
        self.x_in = sem("x_in")
        self.xb_made = sem("xb_made")
        self.xds_made = sem("xds_made")
        self.xt_done = sem("xt_done")
        self.xw_made = sem("xw_made")
        self.y_made = sem("y_made")
        self.yas_made = sem("yas_made")
        self.yd_done = sem("yd_done")
        self.yo_copied = sem("yo_copied")
        self.yo_done = sem("yo_done")
        self.yo_out = sem("yo_out")
        self.yot_done = sem("yot_done")
        self.ysh_made = sem("ysh_made")
        self.ysm_made = sem("ysm_made")
        self.ysplit_done = sem("ysplit_done")
        self.yss_made = sem("yss_made")
        self.yt_copied = sem("yt_copied")
        self.yt_done = sem("yt_done")
        self.ytok_made = sem("ytok_made")
        self.z_in = sem("z_in")
        self.z_out = sem("z_out")
        self.zero_made = sem("zero_made")
        self.zm_made = sem("zm_made")
        self.zt_made = sem("zt_made")


def program(nc, io):
    with ExitStack() as ctx:
        k, s = Core(nc, ctx), Sems(nc, ctx)
        raw_in, psum_free = (s.raw_in0, s.raw_in1), (s.psum_free0, s.psum_free1)
        page_in, state_in, cb_in = (s.page_in0, s.page_in1), (s.hst_in0, s.hst_in1), (s.cb_in0, s.cb_in1)
        tail_out, g_in = (s.tail_out0, s.tail_out1), (s.g_in0, s.g_in1, s.g_in2, s.g_in3)
        v_in = (s.v_in0, s.v_in1, s.v_in2, s.v_in3, s.v_in4)
        ps, ST, CB, YHT, YL, KP, VP = k.ps, k.ST, k.CB, k.YHT, k.YL, k.KP, k.VP
        cache_k, cache_v = (io[n].rearrange("l n t g d -> l n t (g d)") for n in ("cache_k", "cache_v"))
        ident = k.cst[:, K_ID:K_ID + P]
        ones = k.cst[:, K_ONE:K_ONE + P]
        rot = k.cst[:, K_ROT:K_ROT + P]
        w_in = io["w_in"][0].rearrange("(k p) n -> p k n", p=P)

        def dram(name, shape):
            return nc.dram_tensor(name, shape, F32, kind="Internal").ap()

        d_xT = dram("scratch_x", (P, KD, T))
        d_ss = dram("scratch_sample_scores", (72, P))
        d_sm = dram("scratch_sample_mask", (NS, 9 * P))
        d_cum = dram("scratch_cum", (P, P))
        d_dd = dram("scratch_dt", (NS, 2 * HS))
        d_bc = dram("scratch_bc", (NS, 2 * GS * P))
        d_z = dram("scratch_z", (NX, P, T))
        d_g = dram("scratch_gates", (2 * KD, P, T))
        block = ctx.enter_context(nc.Block())

        def pair(o):
            return ps[:, 2 * (o % 2):2 * (o % 2) + 2, 0:HB]

        def halves(ap):
            return ap.rearrange("p (a n) -> p a n", a=2)

        def two_banks(bank):
            return ps[:, bank:bank + 2, :].rearrange("p a n -> p (a n)")[:, 0:T]

        page_table = k.pages[0:1, :].bitcast(I32)

        def load_pages(eng, b, dst, cache, sem, parts=(0, 1)):
            for part in parts:
                first, last = part * NPG // 2, cache.shape[1] - 1
                page = [eng.value_load(page_table[0:1, b * NPG + first + j:b * NPG + first + j + 1], min_val=0, max_val=last) for j in range(NPG // 2)]
                for j in range(NPG // 2):
                    eng.dma_start(dst[:, first + j, :], cache[0, bass.ds(page[j], 1)].rearrange("o t d -> t (o d)")).then_inc(sem, 16)

        def h_hi(t):
            return k.hh[:, t, :]

        def h_lo(t):
            return k.hl[:, t, :]

        def y_hi(t):
            return YHT[t // 4][:, t % 4, :]

        def y_lo(t):
            return YL[t // 4][:, t % 4, :]

        @block.sync
        def _(sp):
            def load(slot, src, cols=P, first=0, nk=KD):
                sp.dma_start(k.raw[:, slot, 0:nk, first:first + cols], src).then_inc(raw_in[slot], 16)

            def unit(u, src, **kw):
                if u >= 2:
                    sp.wait_ge(s.split_done, u - 1)
                load(u % 2, src, **kw)

            def w_view(name):
                return io[name][0].rearrange("(k p) n -> p k n", p=P)

            w_so, w_ao, w_o, w_gu, w_dn = (w_view(n) for n in ("w_ssd_out", "w_attn_out", "w_o", "w_gate_up", "w_down"))

            def unit_source(u):
                if u >= U_WO:
                    return w_o[:, :, (u - U_WO) * P:(u - U_WO + 1) * P]
                if u >= U_AO:
                    return w_ao[:, :, (u - U_AO) * P:(u - U_AO + 1) * P]
                if u >= U_SO:
                    m, half = (u - U_SO) // 2, (u - U_SO) % 2
                    return w_so[:, KD * half:KD * (half + 1), m * P:(m + 1) * P]
                first, u0 = (C_GA, U_G) if u >= U_G else (C_Z, U_Z)
                return w_in[:, :, first + (u - u0) * P:first + (u - u0 + 1) * P]

            def tile_out(o):
                sp.wait_ge(psum_free[o % 2], o // 2 + 1)

            sp.dma_start(k.cst[:, 0:K_UT], io["constants"][:, 0:K_UT]).then_inc(s.x_in, 16)
            for b in range(NBLK):
                sp.dma_start(k.xtok[:, b, :], io["x_prompt"][0, b * P:(b + 1) * P, :]).then_inc(s.x_in, 16)
            sp.dma_start(k.xtoks[0:NS, :], io["x_sample"][:, 0, :]).then_inc(s.x_in, 16)
            sp.dma_start(k.cst[:, K_UT:], io["constants"][:, K_UT:]).then_inc(s.const_in, 16)
            pr = k.tmp[:, :, 0:P]
            for row, slot, src in (
                (0, 0, io["conv_w"][0].rearrange("j (m c) -> (j m) c", c=P)),
                (96, 0, io["conv_b"][0].rearrange("(m c) -> m c", c=P)),
                (120, 0, io["g_mix_pre"][0].rearrange("(m c) -> m c", c=P)),
                (0, 1, io["g_ssd"][0].rearrange("(m c) -> m c", c=P)),
                (16, 1, io["g_mix_post"][0].rearrange("(m c) -> m c", c=P)),
                (24, 1, io["g_ffn_pre"][0].rearrange("(m c) -> m c", c=P)),
                (32, 1, io["g_ffn_post"][0].rearrange("(m c) -> m c", c=P)),
            ):
                sp.dma_start(pr[row:row + src.shape[0], slot, :], src).then_inc(s.const_in, 16)
            for col, n, src in ((0, HS, io["dt_bias"]), (32, HS, io["a_log"]), (64, HS, io["d_skip"]),
                                (96, IDM, io["g_idx_k"]), (160, IDM, io["b_idx_k"])):
                sp.dma_start(k.bcp[:, col:col + n], src.to_broadcast([P, n])).then_inc(s.const_in, 16)
            sp.dma_start(k.csr[0:NS * (CW - 1), :], io["state_conv"][0].rearrange("b j c -> (b j) c")).then_inc(s.state_in, 16)
            load(0, w_in[:, :, C_KI:C_KI + IDM + IH], cols=IDM + IH)
            load(0, w_in[:, :, C_DT:C_DT + HS], cols=HS, first=IDM + IH)
            unit(1, w_in[:, :, C_K:C_K + P])
            sp.dma_start(page_table, io["page_table"].rearrange("b g -> (b g)").unsqueeze(0)).then_inc(s.state_in, 16)
            unit(2, w_in[:, :, C_K + P:C_K + 2 * P])
            unit(3, w_in[:, :, C_V:C_V + P])
            sp.dma_start(io["conv_sample"][0, :, 0:CW - 2, :], io["state_conv"][0, :, 1:CW - 1, :]).then_inc(s.out_done, 16)
            for m in (KD - 2, KD - 1):
                tile_out(O_X0 + m)
            sp.dma_start(d_xT, k.xT[:]).then_inc(s.xT_out, 16)
            unit(4, w_in[:, :, C_V + P:C_V + 2 * P])
            sp.wait_ge(s.state_in, 32)
            sp.wait_ge(s.lo_half_made, KD)
            parts = [(b, part) for b in range(NS) for part in range(2)]
            for m in range(NI + NQ):
                first = C_QI + m * P if m < NI else C_Q + (m - NI) * P
                unit(U_Q + m, w_in[:, :, first:first + P])
                for b, part in parts[m * len(parts) // (NI + NQ):(m + 1) * len(parts) // (NI + NQ)]:
                    load_pages(sp, b, k.ipg[:, b], io["cache_idx_k"], s.idx_in, parts=(part,))
            sp.wait_ge(s.kdup_made, 1)
            kk = k.kdup[:, :, :, 0, :]
            for b in range(NBLK):
                sp.dma_start(io["k_prompt"][0, 0, b * P:(b + 1) * P], kk[:, b]).then_inc(s.out_done, 16)
            sp.dma_start(io["k_sample"][0, :, 0], kk[0:NS, 4]).then_inc(s.out_done, 16)
            sp.wait_ge(s.kv_made, 5)
            sp.dma_start(io["v_prompt"][0, 0].rearrange("(b p) g d -> p b (g d)", p=P), k.vtok[:, 0:NBLK, :]).then_inc(s.out_done, 16)
            sp.dma_start(io["v_sample"][0, :, 0].rearrange("b g d -> b (g d)"), k.vtok[0:NS, 4, :]).then_inc(s.out_done, 16)
            sp.wait_ge(s.ki_made, 1)
            sp.dma_start(io["idx_k_prompt"][0, 0].rearrange("(b p) d -> p b d", p=P), k.kln[:, 0:NBLK, 0, :]).then_inc(s.out_done, 16)
            sp.dma_start(io["idx_k_sample"][0, :, 0], k.kln[0:NS, 4, 0, :]).then_inc(s.out_done, 16)
            early_outs = 10 * 16
            unit(U_X, w_in[:, :, C_XBC:C_XBC + P])
            unit(U_X + 1, w_in[:, :, C_XBC + P:C_XBC + 2 * P])

            sp.wait_ge(s.sct_copied, 1)
            sp.dma_start(d_ss, k.mxb[0:72, :]).then_inc(s.bounce_out, 16)
            sp.wait_ge(s.sdd_made, 1)
            sp.dma_start(d_dd, k.wid[0:NS, :]).then_inc(s.bounce_out, 16)
            sp.wait_ge(s.bounce_out, 2 * 16)
            sp.wait_ge(s.out_done, early_outs)
            sp.dma_start(k.scs[0:NS, :], d_ss.rearrange("(b s) t -> b (s t)", b=NS)).then_inc(s.bounce_in, 16)
            sp.wait_ge(s.bounce_out, 2 * 16)
            sp.dma_start(k.ddb[:], d_dd.rearrange("b h -> (b h)").unsqueeze(0).to_broadcast([P, NS * 2 * HS])).then_inc(s.bounce_in, 16)
            sp.wait_ge(s.cum_made, 2)
            sp.dma_start(d_cum, k.cumt[:]).then_inc(s.bounce_out, 16)
            with sp.Fori(1, NC // 2) as i:
                for j in range(2):
                    sp.wait_ge(s.split_done, U_X + j - 1 + 2 * i)
                    load((U_X + j) % 2, w_in[:, :, bass.ds(C_XBC + j * P + 2 * P * i, P)])
            unit(U_Z, unit_source(U_Z))
            unit(U_Z + 1, unit_source(U_Z + 1))
            for g in range(NC // 4):
                cols = slice(4 * g * P, 4 * (g + 1) * P)
                sp.wait_ge(s.tail_copied, g + 1)
                sp.dma_start(io["conv_prompt"][0, 0, :, cols], k.tailtok[0:CW - 1, g % 2, :]).then_inc(tail_out[g % 2], 16)
                sp.dma_start(io["conv_sample"][0, :, CW - 2, cols], k.tailtok[CW - 1:CW - 1 + NS, g % 2, :]).then_inc(tail_out[g % 2], 16)
            sp.wait_ge(s.tail_copied, NC // 4 + 2)
            sp.dma_start(d_bc, k.bcs[0:NS, :]).then_inc(s.bounce_out, 16)

            h0 = io["state_ssm"][0].rearrange("b (j e) d n -> b (e d) j n", e=2)
            h1 = io["ssm_sample"][0].rearrange("b (j e) d n -> b (e d) j n", e=2)

            def load_state(i):
                sp.dma_start(ST[i % 2][:], h0[i // 2, :, 8 * (i % 2):8 * (i % 2) + 8, :]).then_inc(state_in[i % 2], 16)

            def load_bc(b):
                sp.dma_start(k.bcb[:], d_bc[b:b + 1, :].to_broadcast([P, 2 * GS * P])).then_inc(s.bcb_in, 16)

            load_state(0)
            sp.wait_ge(s.bounce_out, 4 * 16)
            load_bc(0)
            sp.wait_ge(s.xds_made, 1)
            load_state(1)

            def store_state(i):
                sp.wait_ge(s.sh_made, i + 1)
                sp.dma_start(h1[i // 2, :, 8 * (i % 2):8 * (i % 2) + 8, :], ST[i % 2][:]).then_inc(s.state_out, 16)
                if i % 2 == 1 and i // 2 + 1 < NS:
                    load_bc(i // 2 + 1)

            for i in range(NBLK * NKV):
                unit(U_Z + i + 2, unit_source(U_Z + i + 2))
                if i >= 1:
                    store_state(i - 1)
                    if i + 1 < NBLK * NKV:
                        sp.wait_ge(s.state_out, 16 * i)
                        load_state(i + 1)
                tile_out(O_Z + i)
                sp.dma_start(d_z[i], k.zst[:]).then_inc(s.z_out, 16)
            store_state(NBLK * NKV - 1)
            def load_cum(st):
                row = (st % NBLK) * HS + (st // NBLK) * RH
                sp.dma_start(CB[st % 2][:, :], d_cum[row:row + RH, :].rearrange("r l -> (r l)").unsqueeze(0).to_broadcast([P, RH * P])).then_inc(cb_in[st % 2], 16)

            def load_z(g):
                sp.dma_start(k.zg[:], d_z[4 * g:4 * g + 4].rearrange("q p t -> p q t")).then_inc(s.z_in, 16)

            sp.wait_ge(s.state_out, 16 * NBLK * NKV)
            load_cum(0)
            sp.wait_ge(s.smask_made, 1)
            sp.dma_start(d_sm, k.wks[0:NS, :]).then_inc(s.bounce_out, 16)
            sp.wait_ge(s.bounce_out, 5 * 16)
            sp.wait_ge(s.z_out, 16 * NX)
            ssm_prompt = io["ssm_prompt"][0, 0].rearrange("(g q e) d n -> g (e d) q n", q=4, e=2)

            def store_last_state(g):
                sp.wait_ge(s.hst_copied, g + 1)
                sp.dma_start(ssm_prompt[g], k.fin[:]).then_inc(s.fin_out, 16)

            sp.dma_start(k.cumt[0:72, :], d_sm.rearrange("b (e t) -> (b e) t", t=P)).then_inc(s.bounce_in, 16)
            def gate_out(n):
                unit(U_G + n + 2, unit_source(U_G + n + 2))
                tile_out(O_G + n)
                sp.dma_start(d_g[n], k.gst[:]).then_inc(s.g_out, 16)

            for n in BEFORE:
                gate_out(n)
            for st in range(GS * NBLK):
                g, c = st // NBLK, st % NBLK
                if st + 1 < GS * NBLK:
                    if st >= 1:
                        sp.wait_ge(s.yd_done, st)
                    load_cum(st + 1)
                if c == 0 and g >= 1:
                    store_last_state(g - 1)
                if c == 1:
                    if g >= 1:
                        sp.wait_ge(s.zm_made, g)
                    load_z(g)
                if st in STEP_UNIT:
                    gate_out(STEP_UNIT[st])
            store_last_state(GS - 1)
            gate_out(AFTER[0])
            sp.wait_ge(s.zm_made, GS)
            sp.wait_ge(s.yd_done, GS * NBLK)
            load_pages(sp, 0, KP[0], cache_k, page_in[0])
            load_pages(sp, 1, KP[1], cache_k, page_in[1])
            for n in AFTER[1:]:
                gate_out(n)
            def load_gate(n):
                sp.dma_start(k.gl[:, n % 4, :], d_g[n]).then_inc(g_in[n % 4], 16)

            sp.wait_ge(s.g_out, 16 * 2 * KD)
            for n in range(4):
                load_gate(n)
            for n in range(2 * KD):
                unit(U_SO + n + 2, unit_source(U_SO + n + 2))
                if n < 6:
                    if n % 2 == 0:
                        sp.wait_ge(s.kst_done, 4 * (n + 1))
                    load_pages(sp, n - n % 2 + 2, KP[0], cache_k, page_in[0], parts=(n % 2,))
                elif n < 8:
                    if n == 6:
                        sp.wait_ge(s.lo_half_made, L_Y + 4 * GS)
                    load_pages(sp, 0, VP[0], cache_v, v_in[0], parts=(n % 2,))
                elif n < 10:
                    if n == 8:
                        sp.wait_ge(s.kst_done, 4 * NS)
                    load_pages(sp, 2, VP[2], cache_v, v_in[2], parts=(n % 2,))
                elif n < 12:
                    if n == 10:
                        sp.wait_ge(s.lg_done, NS)
                    load_pages(sp, 4, VP[4], cache_v, v_in[4], parts=(n % 2,))
                elif n >= 14:
                    if n == 14:
                        sp.wait_ge(s.sv_done, 2)
                    load_pages(sp, 6, VP[1], cache_v, v_in[1], parts=(n % 2,))
                if n % 2 == 1:
                    tile_out(O_SO + n // 2)
                    load_gate(n // 2 + 4)
            for m in range(KD):
                unit(U_AO + m + 2, unit_source(U_AO + m + 2))
                if m < 4:
                    sp.wait_ge(s.mix_made, m + 1)
                    load_gate(KD + 4 + m)
            for m in range(2, KD):
                unit(U_WO + m, unit_source(U_WO + m))
                if m == 2:
                    sp.wait_ge(s.unit_done, U_WO)
                    sp.dma_start(k.x1[:], d_xT).then_inc(s.bounce_in, 16)
            with sp.Fori(0, NF) as i:
                for j in range(2):
                    sp.wait_ge(s.split_done, U_GU + j - 1 + 2 * i)
                    load((U_GU + j) % 2, w_gu[:, :, bass.ds(DFF * j + P * i, P)])
            with sp.Fori(0, KD // 2) as i:
                for j in range(6):
                    k0, nk = sum(DN_K[:j % 3]), DN_K[j % 3]
                    sp.wait_ge(s.split_done, U_DN + j - 1 + 6 * i)
                    load((U_DN + j) % 2, w_dn[:, k0:k0 + nk, bass.ds(P * (j // 3) + 2 * P * i, P)], nk=nk)
            for n in range(10):
                b, cols = n % 5, slice(4 * P * (n // 5), 4 * P * (n // 5 + 1))
                sp.wait_ge(s.yo_copied, n + 1)
                if b < NBLK:
                    sp.dma_start(io["y_prompt"][0, b * P:(b + 1) * P, cols], k.yout[:, n, :]).then_inc(s.yo_out, 16)
                else:
                    sp.dma_start(io["y_sample"][:, 0, cols], k.yout[0:NS, n, :]).then_inc(s.yo_out, 16)
            sp.wait_ge(s.yo_out, 16 * 10)
            sp.wait_ge(s.fin_out, 16 * GS)

        @block.gpsimd
        def _(pool):
            pool.memset(k.zero[:], 0.0).then_inc(s.zero_made, 1)
            pool.wait_ge(s.zero_made, 1)

            def split(slot, arrived, made, used, cols=P, nk=KD):
                pool.wait_ge(raw_in[slot], arrived)
                if used is not None:
                    pool.wait_ge(s.unit_done, used)
                raw, hi, lo = (t[:, slot, 0:nk, 0:cols] for t in (k.raw, k.wh, k.wl))
                pool.tensor_tensor(hi, raw, k.zero[:].unsqueeze(1).to_broadcast([P, nk, cols]), ALU.add).then_inc(s.hi_made, 1)
                pool.wait_ge(s.hi_made, made)
                pool.tensor_tensor(lo, raw, hi.bitcast(F32), ALU.subtract).then_inc(s.split_done, 1)

            def arrived(u):
                return 16 * (u // 2 + 1 + (u % 2 == 0))

            for u in range(5):
                split(u % 2, arrived(u), u + 1, u - 1 if u >= 2 else None, cols=P if u else NMISC)

            def units(u0, n):
                with pool.Fori(0, n // 2) as i:
                    for j in range(2):
                        u = u0 + j
                        split(u % 2, arrived(u) + 16 * i, u + 1 + 2 * i, u - 1 + 2 * i)

            units(U_Q, U_X + 2 - U_Q)
            units(U_X + 2, NC - 2)
            units(U_Z, 2)
            for i in range(NBLK * NKV):
                b, hf = i // 2, i % 2
                u = U_Z + 2 + i
                split(u % 2, arrived(u), u + 1, u - 1)
                pool.wait_ge(s.bcb_in, 16 * (b + 1))
                if i == 0:
                    pool.wait_ge(s.xds_made, 1)
                else:
                    pool.wait_ge(s.sh_made, i)
                xdt = k.xds[:].rearrange("p (j b) -> p j b", b=NS)[:, 8 * hf:8 * hf + 8, b:b + 1].rearrange("p (g q) o -> p g (q o)", g=2)
                pool.tensor_tensor(k.prods[:].rearrange("p (g q) n -> p g q n", g=2), xdt.unsqueeze(3).to_broadcast([P, 2, 4, NST]),
                                   k.bcb[:, 2 * hf * P:(2 * hf + 2) * P].rearrange("p (g n) -> p g n", g=2).unsqueeze(2).to_broadcast([P, 2, 4, NST]),
                                   ALU.mult).then_inc(s.xb_made, 1)
                pool.wait_ge(s.xb_made, i + 1)
                pool.wait_ge(s.hd_made, i + 1)
                pool.tensor_tensor(ST[i % 2][:], ST[i % 2][:], k.prods[:], ALU.add).then_inc(s.hn_made, 1)
            units(U_G + 2, 2 * KD)
            units(U_SO + 2, 2 * KD + KD)
            units(U_WO + 2, KD)
            pool.wait_ge(s.bounce_in, 4 * 16)
            for m in range(KD):
                pool.wait_ge(s.tmp_made, N_O + m + 1)
                pool.tensor_tensor(k.x1[:, m, :], k.x1[:, m, :], k.ot[:, m, :], ALU.add).then_inc(s.x1_made, 1)
            units(U_GU + 2, 2 * NF - 2)
            with pool.Fori(0, KD // 2) as i:
                for j in range(6):
                    u = U_DN + j
                    split(u % 2, arrived(u) + 48 * i, u + 1 + 6 * i, u - 1 + 6 * i, nk=DN_K[j % 3])
            for m in range(KD // 2):
                pool.wait_ge(s.tmp_made, N_D + m + 1)
                pool.tensor_tensor(k.x1[:, m, :], k.x1[:, m, :], k.dt[:, m, :], ALU.add).then_inc(s.x1_made, 1)

        @block.tensor
        def _(pe):
            def free(o, i=0):
                pe.wait_ge(psum_free[o % 2], o // 2 + i)

            def mm3(out, ah, al, bh, bl, n, first=True, last=True):
                for q, (a, b) in enumerate(((ah, bh), (ah, bl), (al, bh))):
                    for t in range(n):
                        mm = pe.matmul(out, a(t), b(t), start=first and q == 0 and t == 0, stop=last and q == 2 and t == n - 1)
                return mm

            def unit(slot, o, xh, xl, n=KD, k0=0, hs=(0, 1), first=True, last=True, cols=P, ready=None, beside=None):
                if ready is not None:
                    for q, made, x in ((0, s.hi_half_made, xh), (1, s.lo_half_made, xl)):
                        for t in range(n):
                            pe.wait_ge(made, ready + t + 1)
                            for w in ((k.wh, k.wl), (k.wh,))[q]:
                                for h in hs:
                                    mm = pe.matmul(ps[0:cols, 2 * (o % 2) + h, 0:HB], w[:, slot, t, 0:cols], x(k0 + t)[:, h * HB:(h + 1) * HB],
                                                   start=first and q == 0 and t == 0 and w is k.wh, stop=last and q == 1 and t == n - 1)
                            if q == 0 and beside is not None:
                                beside(t)
                    return mm
                for h in hs:
                    mm = mm3(ps[0:cols, 2 * (o % 2) + h, 0:HB], lambda t: k.wh[:, slot, t, 0:cols], lambda t: k.wl[:, slot, t, 0:cols],
                             lambda t: xh(k0 + t)[:, h * HB:(h + 1) * HB], lambda t: xl(k0 + t)[:, h * HB:(h + 1) * HB], n, first, last)
                return mm

            pe.wait_ge(s.x_in, 16 * 6)

            def square_sum(m, src, before=0):
                pe.wait_ge(s.sq_ready, before + m + 1)
                for h in range(2):
                    mm = pe.matmul(ps[:, 5 + h, 0:HB], ones, src[:, m % 2, h * HB:(h + 1) * HB], start=(m == 0), stop=(m == KD - 1))
                mm.then_inc(s.ss_done, 1)

            for m in range(KD):
                if m >= 2:
                    free(m)
                for b in range(NBLK):
                    pe.transpose(ps[:, 2 * (m % 2), b * P:(b + 1) * P], k.xtok[:, b, m * P:(m + 1) * P], ident)
                pe.transpose(ps[:, 2 * (m % 2) + 1, 0:NS], k.xtoks[0:NS, m * P:(m + 1) * P], ident[0:NS, 0:NS]).then_inc(s.xt_done, 1)
                if m >= 1:
                    square_sum(m - 1, k.sq)
            square_sum(KD - 1, k.sq)

            pe.wait_ge(s.const_in, 13 * 16)
            pr = k.tmp[:, :, 0:P]
            pe.transpose(ps[:, 4, 0:P], pr[:, 0, :], ident)
            pe.transpose(ps[:, 4, P:P + 40], pr[0:40, 1, :], ident[0:40, 0:40]).then_inc(s.prm_done, 1)
            pe.wait_ge(s.state_in, 32)
            rows = NS * (CW - 1)
            for m in range(NC):
                if m == 20:
                    pe.wait_ge(s.prm_copied, 1)
                out = ps[:, 7, m * rows:(m + 1) * rows] if m < 20 else ps[:, 4, (m - 20) * rows:(m - 19) * rows]
                tr = pe.transpose(out, k.csr[0:rows, m * P:(m + 1) * P], ident[0:rows, 0:rows])
            tr.then_inc(s.prm_done, 1)
            def turn(u):
                cols = P if u else NMISC
                pe.wait_ge(psum_free[(O_T + u) % 2], (O_T + u) // 2 + 1)
                if u >= 2:
                    pe.wait_ge(s.kv_made, u - 1)
                a = 4 + 2 * (u % 2)
                for b in range(NBLK):
                    pe.transpose(ps[:, a, b * P:b * P + cols], k.kvf[0:cols, u, b * P:(b + 1) * P], ident[0:cols, 0:cols])
                pe.transpose(ps[0:NS, a + 1, 0:cols], k.kvf[0:cols, u, TP:T], ident[0:cols, 0:cols]).then_inc(s.kv_turned, 1)

            pe.wait_ge(s.prm_copied, 2)
            for u in range(5):
                free(O_T + u)
                pe.wait_ge(s.split_done, u + 1)
                unit(u % 2, O_T + u, h_hi, h_lo, cols=P if u else NMISC, ready=None if u else 0).then_inc(s.unit_done, 1)
                if u >= 1:
                    turn(u - 1)
            def query_unit(j, i):
                pe.wait_ge(psum_free[(O_Q + j) % 2], (O_Q + j) // 2 + i)
                pe.wait_ge(s.split_done, U_Q + j + 1 + 2 * i)
                unit((U_Q + j) % 2, O_Q + j, h_hi, h_lo).then_inc(s.unit_done, 1)

            def rotate(j, i):
                pe.wait_ge(psum_free[(O_Q + j) % 2], (O_Q + j) // 2 + 1 + i)
                pe.wait_ge(s.rot_free, 2 * i + j + 1)
                for h in range(2):
                    mm = pe.matmul(ps[:, 5 + h, 0:HB], rot, k.qraw[:, j, h * HB:(h + 1) * HB], start=True, stop=True)
                mm.then_inc(s.rot_done, 1)

            query_unit(0, 0)
            turn(4)
            query_unit(1, 0)
            pe.wait_ge(s.kv_made, 5)
            rotate(0, 0)
            with pe.Fori(1, (NI + NQ) // 2) as i:
                query_unit(0, i)
                rotate(1, i - 1)
                query_unit(1, i)
                rotate(0, i)
            rotate(1, (NI + NQ) // 2 - 1)

            pe.wait_ge(s.kdup_made, 2)
            pe.wait_ge(s.ki_made, 2)
            pe.wait_ge(s.q_made, NI + NQ + 1)
            for g in range(NKV + 1):
                if g >= 2:
                    pe.wait_ge(s.kt_copied, g - 1)
                for b in range(5):
                    rows, bank = (P, 4 + 2 * (g % 2)) if b < 4 else (NS, 5 + 2 * (g % 2))
                    src = (k.kdup[0:rows, b, g] if g < NKV else k.kln[0:rows, b]).rearrange("p c d -> p (c d)")
                    tr = pe.transpose(ps[:, bank, b % 4 * P:b % 4 * P + rows], src, ident[0:rows, 0:rows])
                tr.then_inc(s.kt_done, 1)

            def channel_unit(j):
                free(O_X + j)
                pe.wait_ge(s.split_done, U_X + j + 1)
                unit((U_X + j) % 2, O_X + j, h_hi, h_lo).then_inc(s.unit_done, 1)

            pe.wait_ge(s.kt_copied, NKV + 1)
            pe.wait_ge(s.qsi_made, 1)
            qsi = k.qsi[:].rearrange("p (b n) -> p b n", b=NS)
            def turn_pages(b):
                if b >= 2:
                    pe.wait_ge(s.ipg_copied, b - 1)
                for q in range(NPG // 2):
                    tr = pe.transpose(ps[:, 4 + b % 2, q * P:(q + 1) * P], k.ipg[:, b, 2 * q:2 * q + 2, :].rearrange("p g d -> p (g d)"), ident)
                tr.then_inc(s.ipg_done, 1)

            pe.wait_ge(s.idx_in, 16 * NPG * NS)
            turn_pages(0)
            for b in range(NS):
                if b + 1 < NS:
                    turn_pages(b + 1)
                pe.wait_ge(s.ipg_copied, b + 1)
                for q in range(NPG // 2):
                    mm = pe.matmul(ps[:, 6, (b * NPG + 2 * q) * IH:(b * NPG + 2 * q + 2) * IH], k.kit[:, b % 2, q, :], qsi[:, b, :], start=True, stop=True)
                mm.then_inc(s.dot_done, 1)
            pe.matmul(ps[0:NS, 7, 0:NS * IH], k.kid[0:64, TP:T], qsi[0:64, :, 0:IH], start=True, stop=True).then_inc(s.dot_done, 1)
            pe.wait_ge(s.wid_made, 1)
            pe.matmul(ps[:, 4, 0:NS * IH], k.cst[0:NS, K_ONE:K_ONE + P], k.wid[0:NS, :], start=True, stop=True).then_inc(s.wib_done, 1)
            channel_unit(0)
            pe.wait_ge(s.sct_made, 1)
            pe.transpose(ps[0:72, 5, 0:P], k.sct[:], ident).then_inc(s.sct_done, 1)

            pe.wait_ge(s.dt_step_v, 3)
            pe.wait_ge(s.wib_copied, 1)
            pe.matmul(ps[:, 4, 0:P], k.cst[:, K_UT:K_UT + P], k.dta[:, 0:P], start=True, stop=True)
            pe.matmul(ps[:, 4, P:2 * P], ones, k.dta[:, 0:P], start=True, stop=True).then_inc(s.cum_done, 1)
            channel_unit(1)
            pe.wait_ge(s.cum_made, 1)
            pe.wait_ge(s.sct_copied, 1)
            pe.transpose(ps[:, 5, 0:P], k.cum[:], ident).then_inc(s.cum_done, 1)

            pe.wait_ge(s.cum_made, 2)
            n = 0
            for qb in range(1, NBLK):
                for h in range(IH):
                    if n >= 4:
                        pe.wait_ge(s.rel_made, n - 3)
                    f = 64 * (h % 2)
                    pe.matmul(ps[:, 4 + n % 4, 0:(qb + 1) * P], k.qall[f:f + 64, h // 2, qb * P:(qb + 1) * P], k.kid[f:f + 64, 0:(qb + 1) * P],
                              start=True, stop=True).then_inc(s.isc_done, 1)
                    n += 1

            def projections(u0, o0, n, xh, xl, ready=None, begun=0, beside=None):
                if ready is not None:
                    for j in range(2):
                        free(o0 + j)
                        pe.wait_ge(s.split_done, u0 + j + 1)
                        unit((u0 + j) % 2, o0 + j, xh, xl, ready=None if j else ready, beside=beside).then_inc(s.unit_done, 1)
                with pe.Fori(begun if ready is None else 1, n // 2) as i:
                    for j in range(2):
                        pe.wait_ge(psum_free[(o0 + j) % 2], (o0 + j) // 2 + i)
                        pe.wait_ge(s.split_done, u0 + j + 1 + 2 * i)
                        unit((u0 + j) % 2, o0 + j, xh, xl).then_inc(s.unit_done, 1)

            projections(U_X, O_X, NC, h_hi, h_lo, begun=1)
            free(O_Z)
            pe.wait_ge(s.split_done, U_Z + 1)
            unit(U_Z % 2, O_Z, h_hi, h_lo).then_inc(s.unit_done, 1)
            for g in range(NC // 4):
                if g == 0:
                    pe.wait_ge(s.tail_made, NC)
                    pe.wait_ge(s.rel_made, n)
                if g >= 2:
                    pe.wait_ge(s.tail_copied, g - 1)
                for q in range(4):
                    tr = pe.transpose(ps[0:CW - 1 + NS, 4 + g % 2, q * P:(q + 1) * P], k.tail[:, 4 * g + q, :], ident)
                tr.then_inc(s.tail_done, 1)
            pe.wait_ge(s.conv_made, NC)
            for g in range(2 * GS):
                tr = pe.transpose(ps[0:NS, 6 + g // 4, g % 4 * P:(g % 4 + 1) * P], k.xbc[:, NX + g, TP:T], ident)
            tr.then_inc(s.tail_done, 1)

            def logits(i, heads):
                qb, g = i // NKV, i % NKV
                for r in heads:
                    h = 4 * g + r
                    f = 64 * (h % 2)
                    pe.matmul(ps[:, 4 + r, 0:(qb + 1) * P], k.qall[f:f + 64, NI + h // 2, qb * P:(qb + 1) * P], k.ktd[f:f + 64, g, 0:(qb + 1) * P],
                              start=True, stop=True).then_inc(s.logit_done, 1)

            for i in range(NBLK * NKV):
                qb, g = i // NKV, i % NKV
                kq = (qb + 1) * P
                u, o = U_Z + i, O_Z + i
                if i == 0:
                    pe.wait_ge(s.tail_copied, NC // 4 + 2)
                    logits(0, (2, 3, 0, 1))
                if i >= 1:
                    free(o)
                    pe.wait_ge(s.split_done, u + 1)
                    unit(u % 2, o, h_hi, h_lo, hs=(0,))
                for r in range(4):
                    pe.wait_ge(s.p_made, 4 * i + r + 1)
                    for t in range(qb + 1):
                        tr = pe.transpose(ps[:, 4 + r, t * P:(t + 1) * P], k.sb[:, r, t * P:(t + 1) * P], ident)
                    tr.then_inc(s.pt_done, 1)
                if i >= 1:
                    unit(u % 2, o, h_hi, h_lo, hs=(1,)).then_inc(s.unit_done, 1)
                pe.wait_ge(s.pt_copied, 4 * (i + 1))
                for r in range(4):
                    for t in range(qb + 1):
                        mm = pe.matmul(ps[:, 4, r * HD:(r + 1) * HD], k.pt[:, r, t * P:(t + 1) * P], k.vtok[:, t, g * HD:(g + 1) * HD],
                                       start=(t == 0), stop=(t == qb))
                mm.then_inc(s.av_done, 1)
                if i + 1 < NBLK * NKV:
                    logits(i + 1, (2, 3))
                pe.wait_ge(s.ytok_made, i + 1)
                for q in range(2):
                    tr = pe.transpose(ps[:, 5, q * P:(q + 1) * P], k.yat[:, q * P:(q + 1) * P], ident)
                tr.then_inc(s.yt_done, 1)
                if i + 1 < NBLK * NKV:
                    logits(i + 1, (0,))
                    pe.wait_ge(s.yt_copied, i + 1)
                    logits(i + 1, (1,))

            def y_turn(st):
                pe.wait_ge(s.sy_made, st + 1)
                for q in range(4):
                    tr = pe.transpose(ps[:, 6, q * P:(q + 1) * P], k.sy[:, q * P:(q + 1) * P], ident)
                tr.then_inc(s.syt_done, 1)

            def group_end(g):
                for q in range(4):
                    pe.wait_ge(s.gsq_ready, 4 * g + q + 1)
                    pe.matmul(ps[:, 7, :], ones, k.gsq[:, q % 2, :], start=(q == 0), stop=(q == 3)).then_inc(s.gss_done, 1)

            def state_turn(g):
                pe.wait_ge(s.h_made, 4 * g + 4)
                for q in range(4):
                    tr = pe.transpose(ps[:, 7, q * P:(q + 1) * P], k.hst[:, q * P:(q + 1) * P], ident)
                tr.then_inc(s.hst_done, 1)

            def gate_unit(n, hs=(0, 1)):
                u, o = U_G + n, O_G + n
                if hs[0] == 0:
                    free(o)
                    pe.wait_ge(s.split_done, u + 1)
                mm = unit(u % 2, o, h_hi, h_lo, hs=hs)
                if hs[-1] == 1:
                    mm.then_inc(s.unit_done, 1)

            for n in BEFORE:
                gate_unit(n)
            for st in range(GS * NBLK):
                g, c = st // NBLK, st % NBLK
                cc = slice(c * P, (c + 1) * P)
                n = STEP_UNIT.get(st)
                if st == 2:
                    pe.wait_ge(s.bounce_in, 3 * 16)
                    pe.wait_ge(s.cbm_made, st)
                    pe.wait_ge(s.btok_made, st)
                    pe.transpose(ps[:, 4, 0:72], k.cumt[0:72, :], ident[0:72, 0:72]).then_inc(s.mskt_done, 1)
                    pe.wait_ge(s.msks_made, 1)
                if st == 0:
                    pe.wait_ge(s.yt_copied, NBLK * NKV)
                    pe.wait_ge(s.ysm_made, 1)
                else:
                    pe.wait_ge(s.cbm_made, st)
                    pe.wait_ge(s.btok_made, st)
                    pe.wait_ge(s.h_made, st)
                pe.matmul(ps[:, 4, 0:P], k.xbc[:, NX + g, cc], k.xbc[:, NX + GS + g, cc], start=True, stop=True)
                pe.transpose(ps[:, 4, P:2 * P], k.xbc[:, NX + g, cc], ident).then_inc(s.cb_done, 1)
                for q in range(4):
                    tr = pe.transpose(ps[:, 5, q * P:(q + 1) * P], k.xbc[:, 4 * g + q, cc], ident)
                tr.then_inc(s.sxt_done, 1)
                if st >= 1 and c == 0:
                    pe.wait_ge(s.sy_made, st)
                    state_turn(g - 1)
                if n is not None:
                    gate_unit(n, hs=(0,))
                if st >= 1:
                    y_turn(st - 1)
                if g >= 1 and c == 1:
                    group_end(g - 1)
                if n is not None:
                    gate_unit(n, hs=(1,))
                if st >= 1:
                    pe.wait_ge(s.u_made, st)
                if c > 0:
                    pe.wait_ge(s.h_made, st)
                    pe.matmul(ps[:, 6, :], k.xbc[:, NX + GS + g, cc], k.hst[:], start=True, stop=True).then_inc(s.yo_done, 1)
                pe.wait_ge(s.btok_made, st + 1)
                pe.wait_ge(s.xw_made, st + 1)
                pe.matmul(ps[:, 5, :], k.btok[:], k.xw[:], start=True, stop=True).then_inc(s.cs_done, 1)
                pe.wait_ge(s.m_made, st + 1)
                if st >= 1:
                    pe.wait_ge(s.sy_made, st)
                if g >= 1 and c == 0:
                    pe.wait_ge(s.hst_copied, g)
                if g >= 1 and c == 1:
                    pe.wait_ge(s.gstd_made, g)
                for r in range(RH):
                    mm = pe.matmul(ps[:, 7, r * HDS:(r + 1) * HDS], CB[st % 2][:, r * P:(r + 1) * P], k.xdt[:, r * HDS:(r + 1) * HDS], start=True, stop=True)
                mm.then_inc(s.yd_done, 1)
            y_turn(GS * NBLK - 1)
            state_turn(GS - 1)
            gate_unit(AFTER[0])
            pe.wait_ge(s.usq_made, 1)
            for g in range(GS):
                for q in range(4):
                    mm = pe.matmul(ps[:, 4, g * NS:(g + 1) * NS], ones, k.ysq[:, (4 * g + q) * NS:(4 * g + q + 1) * NS], start=(q == 0), stop=(q == 3))
            mm.then_inc(s.uss_done, 1)
            pe.wait_ge(s.hst_copied, GS)
            group_end(GS - 1)
            for n in AFTER[1:]:
                gate_unit(n)
            pe.wait_ge(s.qsm_made, 1)
            pe.wait_ge(s.ysplit_done, 1)
            pe.wait_ge(s.msks_made, 1)
            qsm = k.qsm[:].rearrange("p (a b h) -> p a b h", a=2, b=NS)
            pr = k.lg[:].rearrange("p (b e h) -> p b e h", b=NS, h=NH)

            def row_keys(b):
                pe.wait_ge(page_in[b % 2], 16 * NPG * (b // 2 + 1))
                if b == 0:
                    pe.wait_ge(s.gstd_made, GS)
                    pe.wait_ge(s.rss_made, 1)
                for q in range(4):
                    if b:
                        pe.wait_ge(s.kst_copied, 4 * (b - 1) + q + 1)
                        if q == 0:
                            pe.wait_ge(s.lg_copied, b)
                    for e in range(4):
                        n = 4 * q + e
                        tr = pe.transpose(ps[:, 4 + q, e * P:(e + 1) * P], KP[b % 2][:, n // 2, n % 2 * P:(n % 2 + 1) * P], ident)
                    tr.then_inc(s.kst_done, 1)

            def row_logits(b):
                pe.wait_ge(s.kst_copied, 4 * (b + 1))
                for g in range(NPG):
                    for a in range(2):
                        mm = pe.matmul(ps[:, 4, g * NH + 8 * a:g * NH + 8 * a + 8], k.kst[:, 2 * g + a, :], qsm[:, a, b, :], start=True, stop=True)
                mm.then_inc(s.lg_done, 1)

            def row_values(b):
                pe.wait_ge(v_in[b % 5], 16 * NPG * (1 + b // 5))
                for a in range(2):
                    out = ps[:, 4, (a * NS + b) * 8:(a * NS + b + 1) * 8]
                    for g in range(NPG):
                        pe.matmul(out, VP[b % 5][:, g, a * P:(a + 1) * P], pr[:, b, g, 8 * a:8 * a + 8], start=(g == 0), stop=False)
                    mm = pe.matmul(out, k.vsn[0:NS, a * P:(a + 1) * P], pr[0:NS, b, NPG, 8 * a:8 * a + 8], start=False, stop=True)
                mm.then_inc(s.sv_done, 1)

            for n in range(2 * KD):
                o = O_SO + n // 2
                if 0 < n < NS:
                    row_keys(n)
                if n == 1:
                    pe.wait_ge(s.lo_half_made, L_Y + 4 * GS)
                if n % 2 == 0:
                    free(o)
                pe.wait_ge(s.split_done, U_SO + n + 1)
                unit((U_SO + n) % 2, o, y_hi, y_lo, k0=KD * (n % 2), first=n % 2 == 0, last=n % 2 == 1).then_inc(s.unit_done, 1)
                if n == 0:
                    row_keys(0)
                if n < NS:
                    row_logits(n)
                if n == NS - 1:
                    pe.wait_ge(s.kst_copied, 4 * NS)
                    for a in range(2):
                        mm = pe.matmul(ps[0:NS, 5, a * 64:(a + 1) * 64], k.kts[:, a * NS:(a + 1) * NS], k.qsm[:, a * 64:(a + 1) * 64], start=True, stop=True)
                    mm.then_inc(s.lg_step_t, 1)
                if n == NS:
                    pe.wait_ge(s.lg_step_v, 2)
                    pe.transpose(ps[:, 6, 0:P], k.mxb[:], ident).then_inc(s.lg_step_t, 1)
                if n == NS + 1:
                    pe.wait_ge(s.lg_step_v, 3)
                    pe.matmul(ps[:, 7, 0:P], ones, k.dgm[:], start=True, stop=True).then_inc(s.lg_step_t, 1)
                if n == NS + 2:
                    pe.wait_ge(s.lg_step_v, 5)
                    pe.matmul(ps[:, 6, 0:P], ones, k.mxb[:], start=True, stop=True).then_inc(s.lg_step_t, 1)
                    pe.wait_ge(s.lg_copied, NS)
                for b in {NS + 3: (0, 1), NS + 4: (2, 3), NS + 5: (4,), NS + 6: (5,), NS + 7: (6,)}.get(n, ()):
                    row_values(b)
            row_values(NS - 1)

            projections(U_AO, O_AO, KD, lambda t: k.yah[:, t, :], lambda t: k.yal[:, t, :], ready=L_A)

            def sums(sq, first):
                for h in range(2):
                    mm = pe.matmul(ps[:, 5 + h, 0:HB], ones, sq[:, h * HB:(h + 1) * HB], start=first, stop=not first)
                return mm

            def first_squares(sq, adds):
                pe.wait_ge(s.sq_added, adds)
                sums(sq[:, 2, :], True).then_inc(s.ss_done, KD - 1)

            def last_squares(sq, before):
                pe.wait_ge(s.sq_ready, before + KD)
                sums(sq[:, (KD - 1) % 2, :], False).then_inc(s.ss_done, 1)

            for m in range(KD):
                free(O_WO + m)
                pe.wait_ge(s.split_done, U_WO + m + 1)
                wo_unit = lambda hs, ready=None: unit((U_WO + m) % 2, O_WO + m, lambda t: k.mh[:, t, :], lambda t: k.ml[:, t, :], hs=hs, ready=ready)
                if m < KD - 1:
                    wo_unit((0, 1), None if m else L_M).then_inc(s.unit_done, 1)
                else:
                    wo_unit((0,))
                    first_squares(k.osq, KD - 2)
                    wo_unit((1,)).then_inc(s.unit_done, 1)
            last_squares(k.osq, Q_O)
            pe.wait_ge(s.std_made, 2)
            def x1_squares(t):
                if t >= 1:
                    square_sum(t - 1, k.osq2, Q_X)
                if t == KD - 1:
                    square_sum(t, k.osq2, Q_X)

            projections(U_GU, O_GU, 2 * NF, lambda t: k.fh[:, t, :], lambda t: k.fl[:, t, :], ready=L_F, beside=x1_squares)

            for m in range(KD):
                free(O_DN + m)
                k0 = 0
                for q, nk in enumerate(DN_K):
                    u = U_DN + 3 * m + q
                    pe.wait_ge(s.split_done, u + 1)
                    if m == 0:
                        pe.wait_ge(s.lo_half_made, L_AH + k0 + nk)
                    unit(u % 2, O_DN + m, lambda t: k.ah[:, t, :], lambda t: k.al[:, t, :], n=nk, k0=k0, first=(q == 0), last=(q == 2)).then_inc(s.unit_done, 1)
                    k0 += nk
                    if m == KD - 1 and q == 0:
                        first_squares(k.dsq, 2 * (KD - 2))
            last_squares(k.dsq, Q_D)
            for q in range(2):
                if q == 0:
                    pe.wait_ge(s.x1_made, KD + KD // 2)
                else:
                    pe.wait_ge(s.y_made, KD // 2)
                for b in range(5):
                    rows, n = P if b < NBLK else NS, 5 * q + b
                    if n >= 8:
                        pe.wait_ge(s.yo_copied, n - 7)
                    for e in range(4):
                        tr = pe.transpose(ps[0:rows, n % 8, e * P:(e + 1) * P], k.x1[:, 4 * q + e, b * P:b * P + rows], ident)
                    tr.then_inc(s.yot_done, 1)

        @block.scalar
        def _(act):
            def run(out, src, func, scale=1.0, bias=0.0, **kw):
                return act.activation(out, src, func, bias=bias, scale=scale, **kw)

            def copy(out, src):
                return act.activation(out, src, ACT.Copy)

            for m in range(KD):
                act.wait_ge(s.xt_done, m + 1)
                copy(k.xT[:, m, :], two_banks(2 * (m % 2))).then_inc(psum_free[m % 2], 1)
            act.wait_ge(s.ss_done, KD)
            act.wait_ge(s.eps_made, 1)
            run(halves(k.rst[:]), ps[:, 5:7, 0:HB], ACT.Sqrt, scale=1.0 / D, bias=k.eps[:]).then_inc(s.std_made, 1)
            act.wait_ge(s.const_in, 13 * 16)
            run(k.neg_a[:], k.bcp[:, 32:64], ACT.Exp).then_inc(s.ea_made, 1)
            act.wait_ge(s.prm_done, 1)
            copy(k.prm[:], ps[:, 4, 0:168]).then_inc(s.prm_copied, 1)
            act.wait_ge(s.prm_done, 2)
            copy(k.stT[:, 0:20, :].rearrange("p m r -> p (m r)"), ps[:, 7, 0:480])
            copy(k.stT[:, 20:24, :].rearrange("p m r -> p (m r)"), ps[:, 4, 0:96]).then_inc(s.prm_copied, 1)
            for m in range(KD):
                act.wait_ge(s.tmp_made, m + 1)
                copy(k.hh[:, m, :], k.tmp[:, m % 2, :]).then_inc(s.hi_half_made, 1)
            def by_feature(u):
                o, cols = O_T + u, P if u else NMISC
                act.wait_ge(s.unit_done, u + 1)
                copy(halves(k.kvf[0:cols, u, :]), pair(o)[0:cols]).then_inc(psum_free[o % 2], 1)

            def by_token(u):
                act.wait_ge(s.kv_turned, u + 1)
                a, cols = 4 + 2 * (u % 2), P if u else NMISC
                dst = k.vtok if u >= 3 else k.ktok if u else k.misc
                first = (u - 1) % 2 * P if u else 0
                copy(dst[:, 0:NBLK, first:first + cols], ps[:, a, :].rearrange("p (b c) -> p b c", b=NBLK)[:, :, 0:cols])
                if u >= 3:
                    copy(k.vsn[0:NS, first:first + cols], ps[0:NS, a + 1, 0:cols])
                copy(dst[0:NS, 4, first:first + cols], ps[0:NS, a + 1, 0:cols]).then_inc(s.kv_made, 1)

            act.wait_ge(s.blank_made, 1)
            by_feature(0)
            by_feature(1)
            by_token(0)
            act.wait_ge(s.var_made, 1)
            run(k.lns[:, 10:15], k.lns[:, 5:10], ACT.Sqrt, scale=1.0 / IDM, bias=k.eps[:]).then_inc(s.kstd_made, 1)
            act.wait_ge(s.dt_step_v, 1)
            run(k.sp1[:], k.sp1[:], ACT.Exp, scale=-1.0).then_inc(s.dt_step_s, 1)
            act.wait_ge(s.dt_step_v, 2)
            run(k.dta[:], k.dts[:], ACT.Ln).then_inc(s.dt_step_s, 1)
            for u in range(2, 5):
                by_feature(u)
                by_token(u - 1)

            def query(o, j, u, before):
                act.wait_ge(s.unit_done, u)
                if before is not None:
                    act.wait_ge(s.q_made, before)
                copy(halves(k.qraw[:, j, :]), pair(o)).then_inc(psum_free[o % 2], 1)

            query(O_Q, 0, U_Q + 1, None)
            by_token(4)
            query(O_Q + 1, 1, U_Q + 2, None)
            with act.Fori(1, (NI + NQ) // 2) as i:
                for j in range(2):
                    query(O_Q + j, j, U_Q + j + 1 + 2 * i, 2 * i + j)
            for g in range(NKV + 1):
                act.wait_ge(s.kt_done, g + 1)
                copy(k.ktd[:, g, :] if g < NKV else k.kid[:], two_banks(4 + 2 * (g % 2))).then_inc(s.kt_copied, 1)
            for b in range(NS):
                act.wait_ge(s.ipg_done, b + 1)
                if b >= 2:
                    act.wait_ge(s.dot_done, b - 1)
                copy(k.kit[:, b % 2].rearrange("p q t -> p (q t)"), ps[:, 4 + b % 2, :]).then_inc(s.ipg_copied, 1)
            act.wait_ge(s.wib_done, 1)
            copy(k.wib[:], ps[:, 4, 0:NS * IH]).then_inc(s.wib_copied, 1)
            act.wait_ge(s.sct_done, 1)
            copy(k.mxb[0:72, :], ps[0:72, 5, 0:P]).then_inc(s.sct_copied, 1)
            act.wait_ge(s.cum_done, 1)
            copy(k.cum[:], ps[:, 4, 0:P])
            run(k.expc[:], ps[:, 4, 0:P], ACT.Exp)
            run(k.dec[:], ps[:, 4, P:2 * P], ACT.Exp).then_inc(s.cum_made, 1)
            copy(k.wid[0:NS, 0:HS], k.dts[0:NS, 4 * HS:5 * HS])
            run(k.wid[0:NS, HS:2 * HS], k.dta[0:NS, 4 * HS:5 * HS], ACT.Exp).then_inc(s.sdd_made, 1)
            act.wait_ge(s.tot_made, 1)
            run(k.wdec[:], k.wdec[:], ACT.Exp).then_inc(s.ew_made, 1)
            act.wait_ge(s.cum_done, 2)
            copy(k.cumt[:], ps[:, 5, 0:P]).then_inc(s.cum_made, 1)
            n = 0
            for qb in range(1, NBLK):
                for h in range(IH):
                    act.wait_ge(s.isc_done, n + 1)
                    if n >= 2:
                        act.wait_ge(s.acc_made, n - 1)
                    run(k.rel[:, n % 2, 0:(qb + 1) * P], ps[:, 4 + n % 4, 0:(qb + 1) * P], ACT.Relu).then_inc(s.rel_made, 1)
                    n += 1

            first, wide = CW - 1 + TP, CW * NS
            own = lambda ap, j: ap[:, first + j:first + wide:CW]
            for j in range(2):
                run(k.cx[:, j, 0:CW - 1], k.cst[:, 0:CW - 1], ACT.Copy, scale=0.0)

            def channels(o, t, u, j, before):
                act.wait_ge(s.unit_done, u)
                if before is not None:
                    act.wait_ge(s.ca_made, before)
                cx = k.cx[:, j, :]
                copy(cx[:, CW - 1:CW - 1 + HB], ps[:, 2 * (o % 2), 0:HB])
                copy(cx[:, CW - 1 + HB:first], ps[:, 2 * (o % 2) + 1, 0:TP - HB])
                copy(own(cx, CW - 1), ps[:, 2 * (o % 2) + 1, TP - HB:HB]).then_inc(psum_free[o % 2], 1)
                copy(cx[:, first:first + wide].rearrange("p (b c) -> p b c", b=NS)[:, :, 0:CW - 1],
                     k.stT[:, bass.ds(t, 1), :].rearrange("p o (b j) -> p (o b) j", b=NS)).then_inc(s.cx_made, 1)

            def silu(t, j, sums):
                act.wait_ge(s.ca_made, sums)
                out = k.xbc[:, bass.ds(t, 1), :].rearrange("p o t -> p (o t)")
                run(out[:, 0:TP], k.ca[:, j, 0:TP], ACT.Silu)
                run(out[:, TP:T], k.ca[:, j, first:TP + wide:CW], ACT.Silu).then_inc(s.conv_made, 1)

            act.wait_ge(s.acc_made, n)
            act.wait_ge(s.prm_copied, 2)
            channels(O_X, 0, U_X + 1, 0, None)
            channels(O_X + 1, 1, U_X + 2, 1, None)
            with act.Fori(0, NC // 2 - 1) as i:
                for j in range(2):
                    silu(2 * i + j, j, CW * (2 * i + j + 1))
                    channels(O_X + j, 2 * i + j + 2, U_X + j + 3 + 2 * i, j, CW * (2 * i + j + 1))
            for j in range(2):
                silu(NC - 2 + j, j, CW * (NC - 1 + j))
            act.wait_ge(s.conv_made, NC)
            for g in range(NC // 4):
                act.wait_ge(s.tail_done, g + 1)
                if g >= 2:
                    act.wait_ge(tail_out[g % 2], 32 * (g // 2))
                copy(k.tailtok[0:CW - 1 + NS, g % 2, :], ps[0:CW - 1 + NS, 4 + g % 2, :]).then_inc(s.tail_copied, 1)
            act.wait_ge(s.tail_done, NC // 4 + 1)
            for j in range(2):
                copy(k.bcs[0:NS, j * 512:(j + 1) * 512], ps[0:NS, 6 + j, :]).then_inc(s.tail_copied, 1)

            for j in range(2):
                act.wait_ge(tail_out[j], 32 * (NC // 8))
            for i in range(NBLK * NKV):
                qb, g = i // NKV, i % NKV
                kq = (qb + 1) * P
                act.wait_ge(s.nb_made, i + 1)
                for r in range(4):
                    run(k.sb[:, r, 0:kq], k.sb[:, r, 0:kq], ACT.Exp, scale=SM_SCALE, bias=k.nb[:, r:r + 1], accum_out=k.sm[:, r:r + 1]).then_inc(s.p_made, 1)
                for r in range(4):
                    act.wait_ge(s.pt_done, 4 * i + r + 1)
                    copy(k.pt[:, r, 0:kq], ps[:, 4 + r, 0:kq]).then_inc(s.pt_copied, 1)
                if i == 0:
                    act.wait_ge(s.xds_made, 1)
                act.wait_ge(state_in[i % 2], 16 * (i // 2 + 1))
                for q in range(8):
                    j = 8 * (i % 2) + q
                    ins = run(ST[i % 2][:, q, :], ST[i % 2][:, q, :], ACT.Copy, scale=k.deb[:, j * NS + i // 2:j * NS + i // 2 + 1])
                ins.then_inc(s.hd_made, 1)
                act.wait_ge(s.unit_done, U_Z + i + 1)
                if i >= 1:
                    act.wait_ge(s.z_out, 16 * i)
                run(halves(k.zst[:]), pair(O_Z + i), ACT.Tanh, scale=0.5).then_inc(s.zt_made, 1)
                act.wait_ge(s.yt_done, i + 1)
                copy(k.qall[:, NI + 2 * g:NI + 2 * g + 2, qb * P:(qb + 1) * P],
                     ps[:, 5, 0:2 * P].rearrange("p (q t) -> p q t", q=2)).then_inc(s.yt_copied, 1)

            def squares(g):
                act.wait_ge(s.zm_made, g + 1)
                if g >= 1:
                    act.wait_ge(s.lo_half_made, L_Y + 4 * g)
                for q in range(4):
                    if q >= 2:
                        act.wait_ge(s.gss_done, 4 * g + q - 1)
                    run(k.gsq[:, q % 2, :], k.xbc[:, 4 * g + q, 0:TP], ACT.Square).then_inc(s.gsq_ready, 1)
                act.wait_ge(s.gss_done, 4 * g + 4)
                run(k.rst[:, 0:TP], ps[:, 7, :], ACT.Sqrt, scale=1.0 / 512, bias=k.eps[:]).then_inc(s.gstd_made, 1)

            def group_hi(g, half):
                for m in (2 * half, 2 * half + 1):
                    act.wait_ge(s.tmp_made, N_Y + 4 * g + m + 1)
                    copy(y_hi(4 * g + m)[:, 0:TP], k.gsq[:, m % 2, :]).then_inc(s.hi_half_made, 1)

            def last_state(g):
                act.wait_ge(s.hst_done, g + 1)
                if g >= 1:
                    act.wait_ge(s.fin_out, 16 * g)
                copy(k.fin[:].rearrange("p q n -> p (q n)"), ps[:, 7, :]).then_inc(s.hst_copied, 1)

            act.wait_ge(s.state_out, 16 * NBLK * NKV)
            def gate(n):
                act.wait_ge(s.unit_done, U_G + n + 1)
                if n >= 1:
                    act.wait_ge(s.g_out, 16 * n)
                run(halves(k.gst[:]), pair(O_G + n), ACT.Tanh, scale=0.5).then_inc(psum_free[(O_G + n) % 2], 1)

            for n in BEFORE:
                gate(n)
            for st in range(GS * NBLK):
                g, c = st // NBLK, st % NBLK
                if st == 2:
                    act.wait_ge(s.mskt_done, 1)
                    copy(k.msks[:], ps[:, 4, 0:72]).then_inc(s.msks_made, 1)
                if g >= 1 and c == 0:
                    last_state(g - 1)
                act.wait_ge(s.cbm_made, st + 1)
                if st >= 1:
                    act.wait_ge(s.cs_done, st)
                copy(k.btok[:], ps[:, 4, P:2 * P]).then_inc(s.btok_made, 1)
                act.wait_ge(s.seg_made, st + 1)
                run(CB[st % 2][:, :], CB[st % 2][:, :], ACT.Exp).then_inc(s.dec_made, 1)
                if g >= 1 and c == 1:
                    squares(g - 1)
                if g >= 1 and c == 3:
                    group_hi(g - 1, 0)
                if g >= 2 and c == 0:
                    group_hi(g - 2, 1)
                if st in STEP_UNIT:
                    gate(STEP_UNIT[st])
            last_state(GS - 1)
            gate(AFTER[0])
            group_hi(GS - 2, 1)
            act.wait_ge(s.uss_done, 1)
            run(k.rss[:], ps[:, 4, 0:32], ACT.Sqrt, scale=1.0 / 512, bias=k.eps[:]).then_inc(s.rss_made, 1)
            act.wait_ge(s.yss_made, 1)
            for g in range(GS):
                ins = copy(YHT[g][:, :, TP:T], k.ysq[:, 32 * g:32 * g + 32].rearrange("p (q b) -> p q b", q=4))
            ins.then_inc(s.ysh_made, 1)
            squares(GS - 1)
            for half in range(2):
                group_hi(GS - 1, half)
            for n in AFTER[1:]:
                gate(n)
            for b in range(NS):
                for q in range(4):
                    act.wait_ge(s.kst_done, 4 * b + q + 1)
                    if b >= 1:
                        act.wait_ge(s.lg_done, b)
                    copy(k.kst[:, 4 * q:4 * q + 4, :].rearrange("p e t -> p (e t)"), ps[:, 4 + q, :]).then_inc(s.kst_copied, 1)
                if 1 <= b <= 6:
                    load_pages(act, (b - 1) // 2 * 2 + 3, KP[1], cache_k, page_in[1], parts=((b - 1) % 2,))
                if b == NS - 1:
                    load_pages(act, 1, VP[1], cache_v, v_in[1])
            act.wait_ge(s.lg_step_v, 4)
            run(k.lg[:], k.lg[:], ACT.Exp, scale=SM_SCALE).then_inc(s.lge_made, 1)
            load_pages(act, 3, VP[3], cache_v, v_in[3])
            act.wait_ge(s.sv_done, 1)
            load_pages(act, 5, VP[0], cache_v, v_in[0])
            act.wait_ge(s.sv_done, 3)
            load_pages(act, 7, VP[2], cache_v, v_in[2])
            act.wait_ge(s.yas_made, 1)
            for m in range(NQ):
                copy(k.yah[:, m, :], k.qall[:, NI + m, :]).then_inc(s.hi_half_made, 1)
            for m in range(KD):
                act.wait_ge(s.mix_made, m + 1)
                run(k.mh[:, m, :], k.mix[:, m, :], ACT.Copy, scale=0.5).then_inc(s.hi_half_made, 1)

            def out_squares(m, o, last_unit, out, sq, added):
                act.wait_ge(s.unit_done, last_unit)
                copy(halves(out[:, m, :]), pair(o)).then_inc(psum_free[o % 2], 1)
                act.wait_ge(psum_free[o % 2], o // 2 + 1)
                if m >= 2:
                    act.wait_ge(s.sq_added, added + max(m - 2, 1))
                run(sq[:, m % 2, :], out[:, m, :], ACT.Square).then_inc(s.sq_ready, 1)

            def sqrt_table():
                run(k.sm[:, 0:1], k.eps[:], ACT.Sqrt)

            def root(sums):
                act.wait_ge(s.ss_done, sums)
                run(halves(k.rst[:]), ps[:, 5:7, 0:HB], ACT.Sqrt, scale=1.0 / D, bias=k.eps[:]).then_inc(s.std_made, 1)

            sqrt_table()
            for m in range(KD):
                out_squares(m, O_WO + m, U_WO + m + 1, k.ot, k.osq, 0)
            root(Q_X)
            for m in range(KD):
                act.wait_ge(s.x1_made, m + 1)
                run(k.fh[:, m, :], k.x1[:, m, :], ACT.Copy, scale=k.prm[:, 152 + m:153 + m]).then_inc(s.hi_half_made, 1)
                if m >= 2:
                    act.wait_ge(s.ss_done, Q_X + m - 1)
                run(k.osq2[:, m % 2, :], k.x1[:, m, :], ACT.Square).then_inc(s.sq_ready, 1)
            root(Q_D)
            with act.Fori(0, NF) as i:
                act.wait_ge(psum_free[O_GU % 2], O_GU // 2 + 1 + i)
                run(k.gs[:], k.gs[:], ACT.Silu).then_inc(s.silu_made, 1)
                act.wait_ge(s.glu_made, i + 1)
                copy(k.ah[:, bass.ds(i, 1), :].rearrange("p o t -> p (o t)"), k.up[:]).then_inc(s.hi_half_made, 1)
            sqrt_table()
            for m in range(KD):
                out_squares(m, O_DN + m, U_DN + 3 * (m + 1), k.dt, k.dsq, KD - 2)
            root(Q_D + KD)
            for n in range(10):
                rows = P if n % 5 < NBLK else NS
                act.wait_ge(s.yot_done, n + 1)
                copy(k.yout[0:rows, n, :], ps[0:rows, n % 8, :]).then_inc(s.yo_copied, 1)

        @block.vector
        def _(dve):
            count = [0]

            def step(ins):
                count[0] += 1
                ins.then_inc(s.dve_step, 1)
                dve.wait_ge(s.dve_step, count[0])

            tt, ts, stt = dve.tensor_tensor, dve.tensor_scalar, dve.scalar_tensor_tensor

            dve.memset(k.eps[:], EPS).then_inc(s.eps_made, 1)
            dve.memset(k.sct[:], NEG)
            dve.memset(k.qsi[:], 0.0)
            dve.memset(k.qsm[:], 0.0)
            dve.memset(k.mx[:], 0.0).then_inc(s.rot_free, 1)
            dve.memset(k.nb[:], 0.0).then_inc(s.q_made, 1)
            for m in range(KD):
                dve.wait_ge(psum_free[m % 2], m // 2 + 1)
                if m >= 2:
                    dve.wait_ge(s.ss_done, m - 1)
                tt(k.sq[:, m % 2, :], k.xT[:, m, :], k.xT[:, m, :], ALU.mult).then_inc(s.sq_ready, 1)
            def norm_split(n, src, gain, rstd, tmp, hi, lo, tmp_made, hi_made, lo_made, n0=0):
                def scaled(m):
                    stt(tmp[:, m % 2, :], src(m), gain(m), rstd, ALU.mult, ALU.mult).then_inc(tmp_made, 1)

                scaled(0)
                for m in range(n):
                    if m + 1 < n:
                        if m >= 1:
                            dve.wait_ge(lo_made, n0 + m)
                        scaled(m + 1)
                    dve.wait_ge(hi_made, n0 + m + 1)
                    tt(lo(m), tmp[:, m % 2, :], hi(m).bitcast(F32), ALU.subtract).then_inc(lo_made, 1)

            dve.wait_ge(s.std_made, 1)
            step(dve.reciprocal(k.rst[:], k.rst[:]))
            dve.wait_ge(s.prm_copied, 1)
            norm_split(KD, lambda m: k.xT[:, m, :], lambda m: k.prm[:, 120 + m:121 + m], k.rst[:], k.tmp,
                       lambda m: k.hh[:, m, :], lambda m: k.hl[:, m, :], s.tmp_made, s.hi_half_made, s.lo_half_made)

            dve.wait_ge(s.prm_done, 2)
            for t in (k.ktok, k.vtok, k.misc):
                ins = dve.memset(t[:, 4, :], 0.0)
            ins.then_inc(s.blank_made, 1)
            dve.wait_ge(s.const_in, 13 * 16)
            skips = k.bcp[:, 64:96].rearrange("p (j e) -> p j e", e=2)
            for e in range(2):
                ins = dve.tensor_copy(k.dcol[64 * e:64 * e + 64, :], skips[64 * e:64 * e + 64, :, e])
            step(ins)
            dve.wait_ge(s.ea_made, 1)
            step(ts(k.neg_a[:], k.neg_a[:], -1.0, None, ALU.mult))

            def rope(src, out, cos, sin, t0, t1):
                lo, hi = slice(0, 32), slice(32, 64)
                tt(t0, src(lo), cos, ALU.mult)
                step(tt(t1, src(hi), sin, ALU.mult))
                step(tt(out(lo), t0, t1, ALU.subtract))
                tt(t0, src(hi), cos, ALU.mult)
                step(tt(t1, src(lo), sin, ALU.mult))
                return tt(out(hi), t0, t1, ALU.add)

            cosk = k.cst[:, K_COSK:K_COSK + 160].rearrange("p (b d) -> p b d", b=5)
            sink = k.cst[:, K_SINK:K_SINK + 160].rearrange("p (b d) -> p b d", b=5)
            cosg, sing = (c.unsqueeze(2).to_broadcast([P, 5, NKV, 32]) for c in (cosk, sink))
            dve.wait_ge(s.kv_made, 1)
            ki = k.misc[:, :, 0:IDM]
            col = lambda n: k.lns[:, 5 * n:5 * n + 5]
            wide = lambda n: col(n).unsqueeze(2).to_broadcast([P, 5, IDM])
            step(dve.tensor_reduce(col(0), ki, AX_X, ALU.add))
            step(ts(col(0), col(0), 1.0 / IDM, None, ALU.mult))
            step(tt(k.klt[:], ki, wide(0), ALU.subtract))
            step(tt(k.kln[:, :, 0, :], k.klt[:], k.klt[:], ALU.mult))
            dve.tensor_reduce(col(1), k.kln[:, :, 0, :], AX_X, ALU.add).then_inc(s.var_made, 1)
            dve.wait_ge(s.kstd_made, 1)
            step(dve.reciprocal(col(3), col(2)))
            step(tt(k.klt[:], k.klt[:], wide(3), ALU.mult))
            step(tt(k.klt[:], k.klt[:], k.bcp[:, 96:160].unsqueeze(1).to_broadcast([P, 5, IDM]), ALU.mult))
            step(tt(k.klt[:], k.klt[:], k.bcp[:, 160:224].unsqueeze(1).to_broadcast([P, 5, IDM]), ALU.add))
            t0, t1 = (k.rt[:, n, 0:160].rearrange("p (b d) -> p b d", b=5) for n in range(2))
            rope(lambda d: k.klt[:, :, d], lambda d: k.kln[:, :, 0, d], cosk, sink, t0, t1).then_inc(s.ki_made, 1)
            dve.wait_ge(s.ki_made, 1)
            dve.tensor_copy(k.kln[:, :, 1, :], k.kln[:, :, 0, :]).then_inc(s.ki_made, 1)
            e, u = k.sp1[:], k.dts[:]
            step(tt(k.sp0[:].rearrange("p (b h) -> p b h", b=5), k.misc[:, :, IDM + IH:NMISC], k.bcp[:, 0:HS].unsqueeze(1).to_broadcast([P, 5, HS]), ALU.add))
            stt(k.sp1[:], k.sp0[:], -1.0, k.sp0[:], ALU.mult, ALU.max).then_inc(s.dt_step_v, 1)
            dve.wait_ge(s.dt_step_s, 1)
            ts(u, e, 1.0, None, ALU.add).then_inc(s.dt_step_v, 1)
            dve.wait_ge(s.dt_step_v, 2)
            step(stt(e, u, -1.0, e, ALU.add, ALU.subtract))
            step(dve.reciprocal(k.rt[:, 0, 0:160], u))
            step(tt(e, e, k.rt[:, 0, 0:160], ALU.mult))
            dve.wait_ge(s.dt_step_s, 2)
            step(tt(e, k.dta[:], e, ALU.subtract))
            step(stt(k.dts[:], k.sp0[:], 0.0, e, ALU.max, ALU.add))
            tt(k.dta[:].rearrange("p (b h) -> p b h", b=5), k.dts[:].rearrange("p (b h) -> p b h", b=5),
               k.neg_a[:].unsqueeze(1).to_broadcast([P, 5, HS]), ALU.mult).then_inc(s.dt_step_v, 1)
            wis = k.wis[:].rearrange("p (b h) -> p b h", b=5)
            step(ts(wis, k.misc[:, :, IDM:IDM + IH], IDX_SCALE, None, ALU.mult))
            tt(k.wid[0:NS, :].rearrange("p (b h) -> p b h", b=NS), k.cst[0:NS, K_DG:K_DG + NS].unsqueeze(2).to_broadcast([NS, NS, IH]),
               wis[0:NS, 4:5, :].to_broadcast([NS, NS, IH]), ALU.mult).then_inc(s.wid_made, 1)
            dve.wait_ge(s.kv_made, 3)
            kg = k.ktok[:].rearrange("p b (g d) -> p b g d", g=NKV)
            t0, t1 = (k.rt[:, n, :].rearrange("p (b g d) -> p b g d", b=5, g=NKV) for n in range(2))
            rope(lambda d: kg[:, :, :, d], lambda d: k.kdup[:, :, :, 0, d], cosg, sing, t0, t1).then_inc(s.kdup_made, 1)
            dve.wait_ge(s.kdup_made, 1)
            for b in range(5):
                ins = dve.tensor_copy(k.kdup[:, b, :, 1, :], k.kdup[:, b, :, 0, :])
            ins.then_inc(s.kdup_made, 1)

            cost, sint = (halves(k.cst[:, c:c + T]) for c in (K_COST, K_SINT))
            with dve.Fori(0, (NI + NQ) // 2) as i:
                for j in range(2):
                    dve.wait_ge(s.rot_done, 2 * i + j + 1)
                    dve.wait_ge(s.q_made, 2 * i + j + 1)
                    tt(halves(k.qt[:, 0, :]), ps[:, 5:7, 0:HB], sint, ALU.mult).then_inc(s.rot_free, 1)
                    tt(k.qt[:, 1, :], k.qraw[:, j, :], k.cst[:, K_COST:K_COST + T], ALU.mult).then_inc(s.qt_made, 1)
                    dve.wait_ge(s.qt_made, 2 * i + j + 1)
                    dve.wait_ge(s.rot_free, 2 * i + j + 2)
                    tt(k.qall[:, bass.ds(2 * i + j, 1), :].rearrange("p o t -> p (o t)"), k.qt[:, 0, :], k.qt[:, 1, :], ALU.add).then_inc(s.q_made, 1)
            dve.wait_ge(s.q_made, NI + NQ + 1)
            for f in range(2):
                for e in range(2):
                    fs, es = slice(64 * f, 64 * f + 64), slice(64 * e, 64 * e + 64)
                    dve.tensor_copy(k.qsi[fs, :].rearrange("p (b g j e) -> p g e b j", b=NS, g=2, e=2)[:, f, e],
                                    k.qall[es, 0:NI, TP:T].rearrange("p j b -> p b j"))
                    ins = dve.tensor_copy(k.qsm[fs, :].rearrange("p (a b f r e) -> p f e a r b", a=2, b=NS, f=2, e=2)[:, f, e],
                                          k.qall[es, NI:NI + NQ, TP:T].rearrange("p (a f r) b -> p f a r b", a=2, f=2)[:, f])
            ins.then_inc(s.qsi_made, 1)
            dve.wait_ge(s.kt_copied, NKV + 1)
            for f in range(2):
                fs = slice(64 * f, 64 * f + 64)
                ins = dve.tensor_copy(k.kts[fs, :].rearrange("p (a b) -> p a b", a=2), k.ktd[fs, f:NKV:2, TP:T])
            ins.then_inc(s.qsm_made, 1)

            dve.wait_ge(s.dot_done, NS + 1)
            dve.wait_ge(s.wib_copied, 1)
            rels = k.rels[:].rearrange("p (b g h) -> p b g h", b=NS, g=NPG)
            step(ts(k.rels[:], ps[:, 6, :], 0.0, None, ALU.max))
            wib = k.wib[:].rearrange("p (b h) -> p b h", b=NS)
            step(tt(rels, rels, wib.unsqueeze(2).to_broadcast([P, NS, NPG, IH]), ALU.mult))
            sct = k.sct[:].rearrange("p (b g) -> p b g", b=NS)
            dve.tensor_reduce(sct[:, :, 0:NPG], rels, AX_X, ALU.add)
            new = k.ysq[0:NS, 0:64].rearrange("p (b h) -> p b h", b=NS)
            step(ts(k.ysq[0:NS, 0:64], ps[0:NS, 7, 0:64], 0.0, None, ALU.max))
            step(tt(new, new, wib[0:NS], ALU.mult))
            step(dve.tensor_reduce(k.lns[0:NS, 20:28], new, AX_X, ALU.add))
            step(tt(k.lns[0:NS, 20:28], k.lns[0:NS, 20:28], k.cst[0:NS, K_DG:K_DG + NS], ALU.mult))
            tt(sct[0:NS, :, NPG], k.lns[0:NS, 20:28], k.cst[0:NS, K_DGN:K_DGN + NS], ALU.add).then_inc(s.sct_made, 1)

            dve.wait_ge(s.cum_made, 1)
            tt(k.wdec[:], ps[:, 4, P:2 * P], k.cum[:], ALU.subtract).then_inc(s.tot_made, 1)
            dve.wait_ge(s.ew_made, 1)
            step(tt(k.wdec[:], k.wdec[:], k.dts[:, 0:P], ALU.mult))

            dve.wait_ge(s.out_done, 10 * 16)
            n = 0
            for qb in range(1, NBLK):
                kq = (qb + 1) * P
                acc = k.sc[:, qb - 1, 0:kq]
                for h in range(IH):
                    w = k.wis[:, qb * IH + h:qb * IH + h + 1]
                    dve.wait_ge(s.rel_made, n + 1)
                    rel = k.rel[:, n % 2, 0:kq]
                    if h == 0:
                        ins = ts(acc, rel, w, None, ALU.mult)
                    else:
                        dve.wait_ge(s.acc_made, n)
                        ins = stt(acc, rel, w, acc, ALU.mult, ALU.add)
                    ins.then_inc(s.acc_made, 1)
                    n += 1
                dve.wait_ge(s.acc_made, n)
                last = k.sc[:, qb - 1, qb * P:kq]
                step(tt(last, last, k.cst[:, K_CAUS:K_CAUS + P], ALU.add))
                step(dve.tensor_copy(k.wk[:, qb - 1, 0:kq], acc))

            for _q in range(3):
                dve.sem_inc(s.tk_rep, 1)
            wcol = lambda j, t: k.prm[:, bass.ds(24 * j + t, 1)]
            tiles, rounds = 6, 4
            width = CW * NS + TP
            dve.wait_ge(s.xT_out, 16)
            with dve.Fori(0, NC // tiles) as i:
                for j in range(tiles):
                    t = tiles * i + j
                    cx, ca = k.cx[:, j % 2, :], k.ca[:, j % 2, :]
                    dve.wait_ge(s.cx_made, t + 1)
                    ts(ca, cx[:, 0:width], wcol(0, t), k.prm[:, bass.ds(96 + t, 1)], ALU.mult, ALU.add).then_inc(s.ca_made, 1)
                    slot = k.tail[:, bass.ds(t, 1), :].rearrange("p o c -> p (o c)")
                    dve.tensor_copy(slot[:, 0:CW - 1], cx[:, TP:TP + CW - 1])
                    dve.tensor_copy(slot[:, CW - 1:], cx[:, TP + 2 * (CW - 1):TP + CW - 1 + CW * NS:CW]).then_inc(s.tail_made, 1)
                    items = [(2 * j + e, k.wk[:, (2 * j + e) % 3, 0:((2 * j + e) % 3 + 2) * P], k.m8[:, 8 * ((2 * j + e) % 3):8 * ((2 * j + e) % 3) + 8]) for e in range(2)]
                    for q in range(1, CW):
                        dve.wait_ge(s.ca_made, CW * t + q)
                        if q == 1:
                            dve.wait_ge(s.tk_rep, 12 * i + 2 * j + 2)
                        if q == 2:
                            dve.wait_ge(s.tk_max, 12 * i + 2 * j + 2)
                        stt(ca, cx[:, q:q + width], wcol(q, t), ca, ALU.mult, ALU.add).then_inc(s.ca_made, 1)
                        for n, wk, m8 in items:
                            if q == 1:
                                dve.max(m8, wk).then_inc(s.tk_max, 1)
                            if q == 2:
                                dve.match_replace(wk, m8, wk, GONE).then_inc(s.tk_rep, 1)
            assert NC // tiles * rounds * 8 == TOPK_P

            def taken(rows, sc, last, out, eq, run, cnt, topk):
                step(ts(out, sc, last, 0.0, ALU.is_gt, ALU.add, accum_out=cnt))
                step(ts(cnt, cnt, -1.0, float(topk), ALU.mult, ALU.add))
                step(ts(eq, sc, last, None, ALU.is_equal))
                step(dve.tensor_tensor_scan(run, eq, eq, 0.0, ALU.add, ALU.max))
                step(stt(eq, run, cnt, eq, ALU.is_le, ALU.mult))
                step(tt(eq, eq, out, ALU.add))
                return ts(out, eq, -NEG, NEG, ALU.mult, ALU.add)

            dve.wait_ge(s.conv_made, NC)
            dve.wait_ge(s.tk_rep, 3 + 12 * NC // tiles)
            at = 0
            for qb in range(1, NBLK):
                kq = (qb + 1) * P
                step(taken(P, k.sc[:, qb - 1, 0:kq], k.m8[:, 8 * qb - 1:8 * qb], k.mask[:, at:at + kq],
                           k.cx[:, 0, 0:kq], k.cx[:, 1, 0:kq], k.thr[:, qb:qb + 1], TOPK_P))
                at += kq

            xs_s = k.xbc[:, 0:NX, TP:T]
            by_tile = lambda t: t[:].rearrange("p (j b) -> p j b", b=NS)

            def sample_prepared():
                dve.wait_ge(s.bounce_in, 2 * 16)
                heads = k.ddb[:].rearrange("p (b v j e) -> p e v j b", b=NS, v=2, e=2)
                for e in range(2):
                    es = slice(64 * e, 64 * e + 64)
                    dve.tensor_copy(k.dtb[es, :].rearrange("p (j b) -> p j b", b=NS), heads[es, e, 0])
                    ins = dve.tensor_copy(k.deb[es, :].rearrange("p (j b) -> p j b", b=NS), heads[es, e, 1])
                step(ins)
                tt(by_tile(k.xds), xs_s, by_tile(k.dtb), ALU.mult).then_inc(s.xds_made, 1)
                dve.wait_ge(s.xds_made, 1)
                dve.wait_ge(s.bounce_in, 2 * 16)
                dve.wait_ge(s.bounce_out, 4 * 16)
                step(dve.tensor_copy(k.wks[0:NS, :], k.scs[0:NS, :]))

            def state_out_products(i):
                b, hf = i // 2, i % 2
                dve.wait_ge(s.hn_made, i + 1)
                for q in range(8):
                    j = 8 * hf + q
                    gg = GS + j // 4
                    ins = dve.tensor_tensor_reduce(k.prods[:, q, :], ST[i % 2][:, q, :], k.bcb[:, gg * P:(gg + 1) * P], 1.0, 0.0, ALU.mult, ALU.add,
                                                   k.ysm[:, j * NS + b:j * NS + b + 1])
                ins.then_inc(s.sh_made, 1)

            masks = [k.cst[:, K_CAUS:K_CAUS + P], k.mask[:, 0:256], k.mask[:, 256:640], k.mask[:, 640:1152]]
            for i in range(NBLK * NKV):
                qb, g = i // NKV, i % NKV
                kq = (qb + 1) * P
                if i >= 1:
                    dve.wait_ge(s.nb_made, i)
                for n, r in enumerate((2, 3, 0, 1)):
                    dve.wait_ge(s.logit_done, 4 * i + n + 1)
                    if i >= 1:
                        dve.wait_ge(s.pt_done, 4 * (i - 1) + r + 1)
                    ins = dve.tensor_tensor_reduce(k.sb[:, r, 0:kq], ps[:, 4 + r, 0:kq], masks[qb], 1.0, GONE, ALU.add, ALU.max, k.mx[:, r:r + 1])
                step(ins)
                if i >= 1:
                    dve.wait_ge(s.p_made, 4 * i)
                ts(k.nb[:, 0:4], k.mx[:, 0:4], -SM_SCALE, None, ALU.mult).then_inc(s.nb_made, 1)
                if i == 0:
                    sample_prepared()
                for q in range(2):
                    if q == 1 and i >= 1:
                        state_out_products(i - 1)
                    step(dve.max(k.m8[0:NS, 24:32], k.wks[0:NS, :]))
                    step(dve.match_replace(k.wks[0:NS, :], k.m8[0:NS, 24:32], k.wks[0:NS, :], GONE))
                dve.wait_ge(s.pt_done, 4 * i + 4)
                if i >= 1:
                    dve.wait_ge(s.ytok_made, i)
                step(dve.reciprocal(k.ri[:, 0:4], k.sm[:, 0:4]))
                dve.wait_ge(s.av_done, i + 1)
                if i >= 1:
                    dve.wait_ge(s.yt_done, i)
                tt(k.yat[:].rearrange("p (r d) -> p r d", r=4), ps[:, 4, 0:4 * HD].rearrange("p (r d) -> p r d", r=4),
                   k.ri[:, 0:4].unsqueeze(2).to_broadcast([P, 4, HD]), ALU.mult).then_inc(s.ytok_made, 1)
                dve.wait_ge(s.zt_made, i + 1)
                stt(halves(k.zst[:]), halves(k.zst[:]), 1.0, pair(O_Z + i), ALU.add, ALU.mult).then_inc(psum_free[(O_Z + i) % 2], 1)
            state_out_products(NBLK * NKV - 1)
            assert NBLK * NKV * 2 * 8 == TOPK_S

            dve.wait_ge(s.pt_copied, 4 * NBLK * NKV)
            dve.wait_ge(s.sh_made, NBLK * NKV)
            taken(NS, k.scs[0:NS, :], k.m8[0:NS, 31:32], k.wks[0:NS, :], k.eqs[0:NS, :], k.runs[0:NS, :], k.thr[0:NS, 4:5], TOPK_S).then_inc(s.smask_made, 1)
            step(tt(by_tile(k.ysq), xs_s, k.dcol[:].unsqueeze(2).to_broadcast([P, NX, NS]), ALU.mult))
            tt(xs_s, by_tile(k.ysq), by_tile(k.ysm), ALU.add).then_inc(s.ysm_made, 1)

            dve.wait_ge(s.ysm_made, 1)
            dve.wait_ge(s.bounce_out, 5 * 16)
            heads = lambda t: t.unsqueeze(2).to_broadcast([P, RH, HDS])
            by_head = lambda t: t.rearrange("p (r d) -> p r d", r=RH)
            def norm_step(g, c):
                def low(m):
                    n = L_Y + 4 * g + m + 1
                    dve.wait_ge(s.hi_half_made, n)
                    tt(y_lo(4 * g + m)[:, 0:TP], k.gsq[:, m % 2, :], y_hi(4 * g + m)[:, 0:TP].bitcast(F32), ALU.subtract).then_inc(s.lo_half_made, 1)

                def scaled(m):
                    stt(k.gsq[:, m % 2, :], k.xbc[:, 4 * g + m, 0:TP], k.prm[:, P + 4 * g + m:P + 4 * g + m + 1], k.rst[:, 0:TP], ALU.mult, ALU.mult).then_inc(s.tmp_made, 1)

                if c == 1:
                    dve.wait_ge(s.gstd_made, g + 1)
                    step(dve.reciprocal(k.rst[:, 0:TP], k.rst[:, 0:TP]))
                if c >= 3:
                    for m in (2 * c - 6, 2 * c - 5):
                        low(m)
                if c == 3:
                    dve.wait_ge(s.lo_half_made, L_Y + 4 * g + 2)
                if c in (2, 3):
                    for m in (2 * c - 4, 2 * c - 3):
                        scaled(m)

            for st in range(GS * NBLK + 1):
                g, c = st // NBLK, st % NBLK
                cc = slice(c * P, (c + 1) * P)
                if st < GS * NBLK:
                    hc = slice(c * HS + g * RH, c * HS + (g + 1) * RH)
                    cb = CB[st % 2][:, :]
                    dve.wait_ge(cb_in[st % 2], 16 * (st // 2 + 1))
                    for r in range(RH):
                        cs = k.cum[:, hc.start + r:hc.start + r + 1]
                        ins = ts(cb[:, r * P:(r + 1) * P], cb[:, r * P:(r + 1) * P], cs, cs, ALU.min, ALU.subtract)
                    ins.then_inc(s.seg_made, 1)
                    dve.wait_ge(s.cb_done, st + 1)
                    if st >= 1:
                        dve.wait_ge(s.m_made, st)
                    tt(k.cbm[:], ps[:, 4, 0:P], k.cst[:, K_UT:K_UT + P], ALU.mult).then_inc(s.cbm_made, 1)
                    dve.wait_ge(s.sxt_done, st + 1)
                    if st >= 1:
                        dve.wait_ge(s.yd_done, st)
                    tt(by_head(k.xdt[:]), by_head(ps[:, 5, :]), heads(k.dts[:, hc]), ALU.mult)
                    tt(by_head(k.xw[:]), by_head(ps[:, 5, :]), heads(k.wdec[:, hc]), ALU.mult).then_inc(s.xw_made, 1)
                if 1 <= st <= GS * NBLK:
                    pg, pc = (st - 1) // NBLK, (st - 1) % NBLK
                    pcc = slice(pc * P, (pc + 1) * P)
                    dve.wait_ge(s.syt_done, st)
                    for q in range(4):
                        xs = k.xbc[:, 4 * pg + q, pcc]
                        ins = stt(xs, xs, k.dcol[:, 4 * pg + q:4 * pg + q + 1], ps[:, 6, q * P:(q + 1) * P], ALU.mult, ALU.add)
                    ins.then_inc(s.u_made, 1)
                if st < GS * NBLK:
                    dve.wait_ge(s.cbm_made, st + 1)
                    dve.wait_ge(s.dec_made, st + 1)
                    tt(cb.rearrange("p (r l) -> p r l", r=RH), cb.rearrange("p (r l) -> p r l", r=RH),
                       k.cbm[:].unsqueeze(1).to_broadcast([P, RH, P]), ALU.mult).then_inc(s.m_made, 1)
                if st >= 1:
                    if pc == NBLK - 1:
                        dve.wait_ge(s.u_made, st)
                        dve.wait_ge(s.z_in, 16 * (pg + 1))
                        us = k.xbc[:, 4 * pg:4 * pg + 4, :]
                        stt(us, us, 0.5, k.zg[:], ALU.mult, ALU.mult).then_inc(s.zm_made, 1)
                if st < GS * NBLK:
                    if c > 0:
                        dve.wait_ge(s.yo_done, st - g)
                        dve.wait_ge(s.sy_made, st)
                        step(tt(by_head(k.yt[:]), by_head(ps[:, 6, :]), heads(k.expc[:, hc]), ALU.mult))
                        dve.wait_ge(s.h_made, st)
                        step(tt(by_head(k.hst[:]), by_head(k.hst[:]), heads(k.dec[:, hc]), ALU.mult))
                        dve.wait_ge(s.cs_done, st + 1)
                        tt(k.hst[:], k.hst[:], ps[:, 5, :], ALU.add).then_inc(s.h_made, 1)
                        dve.wait_ge(s.yd_done, st + 1)
                        tt(k.sy[:], k.yt[:], ps[:, 7, :], ALU.add).then_inc(s.sy_made, 1)
                    else:
                        dve.wait_ge(s.cs_done, st + 1)
                        if g >= 1:
                            dve.wait_ge(s.hst_done, g)
                        dve.tensor_copy(k.hst[:], ps[:, 5, :]).then_inc(s.h_made, 1)
                        dve.wait_ge(s.yd_done, st + 1)
                        dve.tensor_copy(k.sy[:], ps[:, 7, :]).then_inc(s.sy_made, 1)
                if g >= 1 and 1 <= c < NBLK:
                    norm_step(g - 1, c)
                if st == GS * NBLK:
                    dve.wait_ge(s.zm_made, GS)
                    tt(by_tile(k.ysq), xs_s, xs_s, ALU.mult).then_inc(s.usq_made, 1)
                if g >= 2 and c == 0:
                    norm_step(g - 2, NBLK)
            dve.wait_ge(s.rss_made, 1)
            step(dve.reciprocal(k.rss[:], k.rss[:]))
            by_group = lambda t: t.rearrange("p (g q b) -> p g q b", g=GS, q=4)
            step(tt(by_tile(k.ysq), xs_s, k.prm[:, P:P + NX].unsqueeze(2).to_broadcast([P, NX, NS]), ALU.mult))
            tt(by_group(k.ysq[:]), by_group(k.ysq[:]), k.rss[:].rearrange("p (g b) -> p g b", g=GS).unsqueeze(2).to_broadcast([P, GS, 4, NS]),
               ALU.mult).then_inc(s.yss_made, 1)
            dve.wait_ge(s.ysh_made, 1)
            for g in range(GS):
                sl = by_tile(k.ysq)[:, 4 * g:4 * g + 4, :]
                ins = tt(YL[g][:, :, TP:T], sl, YHT[g][:, :, TP:T].bitcast(F32), ALU.subtract)
            ins.then_inc(s.ysplit_done, 1)
            for c in (1, 2, 3, 4):
                norm_step(GS - 1, c)

            lg = k.lg[:].rearrange("p (b e h) -> p b e h", b=NS, h=NH)
            dve.memset(lg[:, :, NPG, :], NEG).then_inc(s.lg_step_v, 1)
            msk = k.msks[:].rearrange("p (b e) -> p b e", b=NS)
            dve.wait_ge(s.msks_made, 1)
            own = k.cst[0:NS, K_DGN:K_DGN + NS].unsqueeze(2).to_broadcast([NS, NS, NH])
            new = lg[0:NS, :, NPG, :]
            bh = lambda t: t.rearrange("p (b h) -> p b h", b=NS)
            for n in range(2 * KD):
                if n < NS:
                    dve.wait_ge(s.lg_done, n + 1)
                    tt(lg[:, n, 0:NPG, :], ps[:, 4, 0:P].rearrange("p (e h) -> p e h", h=NH), msk[:, n, 0:NPG].unsqueeze(2).to_broadcast([P, NPG, NH]),
                       ALU.add).then_inc(s.lg_copied, 1)
                if n == NS - 1:
                    dve.wait_ge(s.lg_step_t, 1)
                    dve.wait_ge(s.lg_step_v, 1)
                    step(tt(new.rearrange("p b (a h) -> p b a h", a=2), ps[0:NS, 5, 0:P].rearrange("p (a b h) -> p b a h", a=2, b=NS),
                            own.rearrange("p b (a h) -> p b a h", a=2), ALU.add))
                    step(tt(new, new, msk[0:NS, :, NPG].unsqueeze(2).to_broadcast([NS, NS, NH]), ALU.add))
                    dve.wait_ge(s.lg_copied, NS)
                    dve.tensor_reduce(bh(k.mxb[:]), k.lg[:].rearrange("p (b e h) -> p b h e", b=NS, h=NH), AX_X, ALU.max).then_inc(s.lg_step_v, 1)
                if n == NS:
                    dve.wait_ge(s.lg_step_t, 2)
                    step(dve.tensor_reduce(k.thr[:, 5:6], ps[:, 6, 0:P], AX_X, ALU.max))
                    ts(k.dgm[:], ident, k.thr[:, 5:6], None, ALU.mult).then_inc(s.lg_step_v, 1)
                if n == NS + 1:
                    dve.wait_ge(s.lg_step_t, 3)
                    step(dve.tensor_copy(k.mxb[:], ps[:, 7, 0:P]))
                    tt(lg, lg, bh(k.mxb[:]).unsqueeze(2).to_broadcast([P, NS, NPG + 1, NH]), ALU.subtract).then_inc(s.lg_step_v, 1)
                    dve.wait_ge(s.lge_made, 1)
                    dve.tensor_reduce(bh(k.mxb[:]), k.lg[:].rearrange("p (b e h) -> p b h e", b=NS, h=NH), AX_X, ALU.add).then_inc(s.lg_step_v, 1)
                if n == NS + 2:
                    dve.wait_ge(s.lg_step_t, 4)
                    step(dve.reciprocal(k.rsb[:], ps[:, 6, 0:P]))
                if n % 2 == 1:
                    m, o = n // 2, O_SO + n // 2
                    dve.wait_ge(s.unit_done, U_SO + n + 1)
                    dve.wait_ge(g_in[m % 4], 16 * (m // 4 + 1))
                    stt(halves(k.mix[:, m, :]), halves(k.gl[:, m % 4, :]), 1.0, pair(o), ALU.add, ALU.mult).then_inc(psum_free[o % 2], 1)
            dve.wait_ge(s.sv_done, NS)
            rsb = k.rsb[:].rearrange("p (b a f r e) -> p f e b a r", b=NS, a=2, f=2, r=2)
            for f in range(2):
                for e in range(2):
                    for a in range(2):
                        fs, es = slice(64 * f, 64 * f + 64), slice(64 * e, 64 * e + 64)
                        o8 = ps[fs, 4, a * 64:(a + 1) * 64].rearrange("p (b f r e) -> p f e r b", b=NS, f=2, r=2)[:, f, e]
                        ins = tt(k.qall[es, NI + 4 * a + 2 * f:NI + 4 * a + 2 * f + 2, TP:T], o8, rsb[fs, f, e, :, a, :].rearrange("p b r -> p r b"), ALU.mult)
            ins.then_inc(s.yas_made, 1)
            for m in range(NQ):
                dve.wait_ge(s.hi_half_made, L_A + m + 1)
                tt(k.yal[:, m, :], k.qall[:, NI + m, :], k.yah[:, m, :].bitcast(F32), ALU.subtract).then_inc(s.lo_half_made, 1)
            for m in range(KD):
                o = O_AO + m
                dve.wait_ge(s.unit_done, U_AO + m + 1)
                dve.wait_ge(g_in[m % 4], 16 * ((KD + m) // 4 + 1))
                gl = k.gl[:, (KD + m) % 4, :]
                stt(halves(gl), halves(gl), 1.0, pair(o), ALU.add, ALU.mult).then_inc(psum_free[o % 2], 1)
                dve.wait_ge(psum_free[o % 2], o // 2 + 1)
                tt(k.mix[:, m, :], k.mix[:, m, :], gl, ALU.add).then_inc(s.mix_made, 1)
                dve.wait_ge(s.hi_half_made, L_M + m + 1)
                stt(k.ml[:, m, :], k.mix[:, m, :], 0.5, k.mh[:, m, :].bitcast(F32), ALU.mult, ALU.subtract).then_inc(s.lo_half_made, 1)

            def x1_low(m):
                dve.wait_ge(s.hi_half_made, L_F + m + 1)
                stt(k.fl[:, m, :], k.x1[:, m, :], k.prm[:, 152 + m:153 + m], k.fh[:, m, :].bitcast(F32), ALU.mult, ALU.subtract).then_inc(s.lo_half_made, 1)

            def squares_added(sq, before, added):
                for m in range(1, KD - 1):
                    dve.wait_ge(s.sq_ready, before + m + 1)
                    if m >= 2:
                        dve.wait_ge(s.sq_added, added + m - 1)
                    tt(sq[:, 2, :], sq[:, m % 2, :], sq[:, 2, :] if m >= 2 else sq[:, 0, :], ALU.add).then_inc(s.sq_added, 1)

            squares_added(k.osq, Q_O, 0)
            dve.wait_ge(s.std_made, 2)
            step(dve.reciprocal(k.rst[:], k.rst[:]))
            for m in range(KD):
                stt(k.ot[:, m, :], k.ot[:, m, :], k.prm[:, 144 + m:145 + m], k.rst[:], ALU.mult, ALU.mult).then_inc(s.tmp_made, 1)
                if m >= 1:
                    x1_low(m - 1)
            x1_low(KD - 1)
            dve.wait_ge(s.std_made, 3)
            step(dve.reciprocal(k.rst[:], k.rst[:]))
            with dve.Fori(0, NF) as i:
                o = O_GU + 1
                dve.wait_ge(s.lo_half_made, L_AH + i)
                dve.wait_ge(s.unit_done, U_GU + 1 + 2 * i)
                tt(halves(k.gs[:]), halves(k.rst[:]), pair(O_GU), ALU.mult).then_inc(psum_free[O_GU % 2], 1)
                dve.wait_ge(s.unit_done, U_GU + 2 + 2 * i)
                tt(halves(k.up[:]), halves(k.rst[:]), pair(o), ALU.mult).then_inc(psum_free[o % 2], 1)
                dve.wait_ge(psum_free[o % 2], o // 2 + 1 + i)
                dve.wait_ge(s.silu_made, i + 1)
                tt(k.up[:], k.up[:], k.gs[:], ALU.mult).then_inc(s.glu_made, 1)
                dve.wait_ge(s.hi_half_made, L_AH + i + 1)
                tt(k.al[:, bass.ds(i, 1), :].rearrange("p o t -> p (o t)"), k.up[:],
                   k.ah[:, bass.ds(i, 1), :].rearrange("p o t -> p (o t)").bitcast(F32), ALU.subtract).then_inc(s.lo_half_made, 1)
            squares_added(k.dsq, Q_D, KD - 2)
            dve.wait_ge(s.std_made, 4)
            step(dve.reciprocal(k.rst[:], k.rst[:]))
            for m in range(KD):
                stt(k.dt[:, m, :], k.dt[:, m, :], k.prm[:, 160 + m:161 + m], k.rst[:], ALU.mult, ALU.mult).then_inc(s.tmp_made, 1)
                if m >= KD // 2:
                    dve.wait_ge(s.tmp_made, N_D + m + 1)
                    tt(k.x1[:, m, :], k.x1[:, m, :], k.dt[:, m, :], ALU.add).then_inc(s.y_made, 1)


OUTPUTS = (
    ("y_prompt", (1, TP, D)), ("y_sample", (NS, 1, D)),
    ("k_prompt", (1, 1, TP, NKV, HD)), ("v_prompt", (1, 1, TP, NKV, HD)), ("idx_k_prompt", (1, 1, TP, IDM)),
    ("ssm_prompt", (1, 1, HS, HDS, NST)), ("conv_prompt", (1, 1, CW - 1, CD)),
    ("k_sample", (1, NS, 1, NKV, HD)), ("v_sample", (1, NS, 1, NKV, HD)), ("idx_k_sample", (1, NS, 1, IDM)),
    ("ssm_sample", (1, NS, HS, HDS, NST)), ("conv_sample", (1, NS, CW - 1, CD)),
)


def kernel(**inputs):
    import concourse.bacc as bacc
    from concourse.bass_utils import run_bass_kernel_spmd

    nc = bacc.Bacc("TRN2", target_bir_lowering=False, num_devices=1)
    arrays, io = {}, {}
    for name, value in list(inputs.items()) + [("constants", constants())]:
        a = np.ascontiguousarray(value)
        arrays["in_" + name] = a
        io[name] = nc.dram_tensor("in_" + name, a.shape, mybir.dt.from_np(a.dtype), kind="ExternalInput").ap()
    for name, shape in OUTPUTS:
        io[name] = nc.dram_tensor("out_" + name, shape, F32, kind="ExternalOutput").ap()
    program(nc, io)
    result = run_bass_kernel_spmd(nc, [arrays], core_ids=[0]).results[0]
    return tuple(result["out_" + name] for name, _ in OUTPUTS)
```
